# Optimizing a Trainium2 kernel written in Bass

```python
import jax, jax.numpy as jnp
from jax import lax
import numpy as np

D_MODEL = 1024
BATCH = 1
SEQ = 1024
DEPTH = 2

N_MIXERS = 4
NORM_EPS = 1e-6
ROPE_THETA = 10000.0
LIN_CHUNK = 64
ATTN_BLOCK = 128
HGRN_EXPAND = 128
HGRN_HEADS = D_MODEL // HGRN_EXPAND
HGRN_DK = HGRN_EXPAND
HGRN_DV = D_MODEL // HGRN_HEADS
GLA_HEADS = 4
GLA_KEY_DIM = D_MODEL // 2
GLA_VALUE_DIM = D_MODEL
GLA_DK = GLA_KEY_DIM // GLA_HEADS
GLA_DV = GLA_VALUE_DIM // GLA_HEADS
GLA_GATE_RANK = 16
GLA_GATE_NORMALIZER = 16.0
RET_HEADS = 8
RET_DK = D_MODEL // RET_HEADS
RET_DV = 2 * D_MODEL // RET_HEADS
MLA_HEADS = 8
MLA_Q_LORA = 384
MLA_KV_LORA = 128
MLA_NOPE = 128
MLA_ROPE = 64
MLA_V = 128
MLA_QK = MLA_NOPE + MLA_ROPE
FFN_HIDDEN = -(-8 * D_MODEL // (3 * 256)) * 256

kernel_name = "hybrid_hgrn2_gla_retnet_mla_trunk"

def _rms_norm(x, gain=None):
    xf = x.astype(jnp.float32)
    y = xf * lax.rsqrt(jnp.mean(jnp.square(xf), axis=-1, keepdims=True) + NORM_EPS)
    if gain is not None:
        y = y * gain.astype(jnp.float32)
    return y.astype(x.dtype)

def _rope(x, positions):
    d = x.shape[-1]
    half = d // 2
    inv_freq = 1.0 / (ROPE_THETA ** (jnp.arange(half, dtype=jnp.float32) / half))
    ang = positions.astype(jnp.float32)[..., None] * inv_freq
    cos = jnp.cos(ang)[:, :, None, :]
    sin = jnp.sin(ang)[:, :, None, :]
    xf = x.astype(jnp.float32)
    x1, x2 = xf[..., :half], xf[..., half:]
    return jnp.concatenate([x1 * cos - x2 * sin, x2 * cos + x1 * sin], axis=-1).astype(x.dtype)

def _to_heads(t, n_heads):
    b, s, _ = t.shape
    return t.reshape(b, s, n_heads, -1).transpose(0, 2, 1, 3)

def _to_chunks(t, chunk):
    b, h, l, d = t.shape
    return jnp.moveaxis(t.reshape(b, h, l // chunk, chunk, d), 2, 0)

def _from_chunks(t):
    n, b, h, c, d = t.shape
    return jnp.moveaxis(t, 0, 2).reshape(b, h, n * c, d)

def _gated_linear_scan(q, k, v, log_f):
    b, h, _, dk = q.shape
    dv = v.shape[-1]
    f32 = jnp.float32
    qc, kc, vc, gc = (_to_chunks(t.astype(f32), LIN_CHUNK) for t in (q, k, v, log_f))
    causal = jnp.tril(jnp.ones((LIN_CHUNK, LIN_CHUNK), dtype=bool))[:, :, None]

    def step(state, inp):
        q_, k_, v_, g_ = inp
        cum = jnp.cumsum(g_, axis=2)
        diff = cum[:, :, :, None, :] - cum[:, :, None, :, :]
        decay = jnp.exp(jnp.where(causal, diff, -jnp.inf))
        scores = jnp.einsum('bhtk,bhsk,bhtsk->bhts', q_, k_, decay)
        o_intra = jnp.einsum('bhts,bhsv->bhtv', scores, v_)
        o_inter = jnp.einsum('bhtk,bhkv->bhtv', q_ * jnp.exp(cum), state)
        last = cum[:, :, -1:, :]
        new_state = (jnp.exp(last[:, :, 0, :])[..., None] * state
                     + jnp.einsum('bhsk,bhsv->bhkv', k_ * jnp.exp(last - cum), v_))
        return new_state, o_intra + o_inter

    s0 = jnp.zeros((b, h, dk, dv), f32)
    _, o = lax.scan(step, s0, (qc, kc, vc, gc))
    return _from_chunks(o)

def _retention_scan(q, k, v, log_gamma):
    b, h, _, dk = q.shape
    dv = v.shape[-1]
    f32 = jnp.float32
    qc, kc, vc = (_to_chunks(t.astype(f32), LIN_CHUNK) for t in (q, k, v))
    idx = jnp.arange(LIN_CHUNK, dtype=f32)
    lg = log_gamma[:, None]
    causal = jnp.tril(jnp.ones((LIN_CHUNK, LIN_CHUNK), dtype=bool))
    intra_decay = jnp.exp(jnp.where(causal, lg[:, :, None] * (idx[:, None] - idx[None, :]), -jnp.inf))
    q_decay = jnp.exp(lg * (idx + 1.0))[:, :, None]
    k_decay = jnp.exp(lg * (LIN_CHUNK - 1.0 - idx))[:, :, None]
    chunk_decay = jnp.exp(log_gamma * LIN_CHUNK)[:, None, None]

    def step(state, inp):
        q_, k_, v_ = inp
        scores = jnp.einsum('bhtk,bhsk->bhts', q_, k_) * intra_decay
        o = (jnp.einsum('bhts,bhsv->bhtv', scores, v_)
             + jnp.einsum('bhtk,bhkv->bhtv', q_ * q_decay, state))
        new_state = chunk_decay * state + jnp.einsum('bhsk,bhsv->bhkv', k_ * k_decay, v_)
        return new_state, o

    s0 = jnp.zeros((b, h, dk, dv), f32)
    _, o = lax.scan(step, s0, (qc, kc, vc))
    return _from_chunks(o)

def _causal_attention_blocked(q, k, v):
    b, s, h, dq = q.shape
    dv = v.shape[-1]
    nb = s // ATTN_BLOCK
    scale = dq ** -0.5
    qb = jnp.moveaxis(q.reshape(b, nb, ATTN_BLOCK, h, dq), 1, 0)
    kpos = jnp.arange(s)

    def one_block(args):
        q_blk, j = args
        qpos = j * ATTN_BLOCK + jnp.arange(ATTN_BLOCK)
        sc = jnp.einsum('bqhd,bkhd->bhqk', q_blk, k).astype(jnp.float32) * scale
        sc = jnp.where(kpos[None, :] <= qpos[:, None], sc, -jnp.inf)
        p = jax.nn.softmax(sc, axis=-1).astype(v.dtype)
        return jnp.einsum('bhqk,bkhd->bqhd', p, v)

    o = lax.map(one_block, (qb, jnp.arange(nb)))
    return jnp.moveaxis(o, 0, 1).reshape(b, s, h, dv)

def _hgrn2(h, w_in, g_norm, w_out, lower_bound):
    b, s, _ = h.shape
    q, f, i, g = jnp.split(h @ w_in, 4, axis=-1)
    q = jax.nn.silu(q) * (HGRN_DK ** -0.5)
    forget = lower_bound + (1.0 - lower_bound) * jax.nn.sigmoid(f.astype(jnp.float32))
    k = 1.0 - forget
    log_f = jnp.log(forget)
    o = _gated_linear_scan(_to_heads(q, HGRN_HEADS), _to_heads(k, HGRN_HEADS),
                           _to_heads(i, HGRN_HEADS), _to_heads(log_f, HGRN_HEADS))
    o = o.transpose(0, 2, 1, 3).astype(h.dtype)
    o = _rms_norm(o, g_norm) * jax.nn.silu(g.reshape(b, s, HGRN_HEADS, HGRN_DV))
    return o.reshape(b, s, -1) @ w_out

def _gla(h, w_in, w_gk_up, b_gk, g_norm, w_out):
    b, s, _ = h.shape
    q, k, v, g, gk_low = jnp.split(
        h @ w_in, [GLA_KEY_DIM, 2 * GLA_KEY_DIM, 2 * GLA_KEY_DIM + GLA_VALUE_DIM,
                   2 * GLA_KEY_DIM + 2 * GLA_VALUE_DIM], axis=-1)
    log_f = jax.nn.log_sigmoid((gk_low @ w_gk_up + b_gk).astype(jnp.float32)) / GLA_GATE_NORMALIZER
    q = q * (GLA_DK ** -0.5)
    o = _gated_linear_scan(_to_heads(q, GLA_HEADS), _to_heads(k, GLA_HEADS),
                           _to_heads(v, GLA_HEADS), _to_heads(log_f, GLA_HEADS))
    o = o.transpose(0, 2, 1, 3).astype(h.dtype)
    o = _rms_norm(o, g_norm) * jax.nn.silu(g.reshape(b, s, GLA_HEADS, GLA_DV))
    return o.reshape(b, s, -1) @ w_out

def _retnet(h, positions, w_in, w_out):
    b, s, _ = h.shape
    q, k, v, g = jnp.split(h @ w_in, [D_MODEL, 2 * D_MODEL, 4 * D_MODEL], axis=-1)
    q = _rope(q.reshape(b, s, RET_HEADS, RET_DK), positions)
    k = _rope(k.reshape(b, s, RET_HEADS, RET_DK), positions) * (RET_DK ** -0.5)
    log_gamma = jnp.log(1.0 - 2.0 ** (-5.0 - jnp.arange(RET_HEADS, dtype=jnp.float32)))
    o = _retention_scan(q.transpose(0, 2, 1, 3), k.transpose(0, 2, 1, 3),
                        _to_heads(v, RET_HEADS), log_gamma)
    o = _rms_norm(o.transpose(0, 2, 1, 3).astype(h.dtype))
    o = jax.nn.silu(g) * o.reshape(b, s, -1)
    return o @ w_out

def _mla(h, positions, w_in, g_q_lora, g_kv_lora, w_uq, w_ukv, g_qnorm, g_knorm, w_out):
    b, s, _ = h.shape
    c_q, c_kv, k_rope = jnp.split(h @ w_in, [MLA_Q_LORA, MLA_Q_LORA + MLA_KV_LORA], axis=-1)
    c_q = _rms_norm(c_q, g_q_lora)
    c_kv = _rms_norm(c_kv, g_kv_lora)
    q = (c_q @ w_uq).reshape(b, s, MLA_HEADS, MLA_QK)
    kv = (c_kv @ w_ukv).reshape(b, s, MLA_HEADS, MLA_NOPE + MLA_V)
    k_nope, v = kv[..., :MLA_NOPE], kv[..., MLA_NOPE:]
    k_rope = jnp.broadcast_to(k_rope[:, :, None, :], (b, s, MLA_HEADS, MLA_ROPE))
    k = jnp.concatenate([k_nope, k_rope], axis=-1)
    q = _rms_norm(q, g_qnorm)
    k = _rms_norm(k, g_knorm)
    q = jnp.concatenate([q[..., :MLA_NOPE], _rope(q[..., MLA_NOPE:], positions)], axis=-1)
    k = jnp.concatenate([k[..., :MLA_NOPE], _rope(k[..., MLA_NOPE:], positions)], axis=-1)
    o = _causal_attention_blocked(q, k, v)
    return o.reshape(b, s, -1) @ w_out

def _swiglu(h, w_gate_up, w_down):
    a, u = jnp.split(h @ w_gate_up, 2, axis=-1)
    return (jax.nn.silu(a) * u) @ w_down

def setup_inputs(seed: int = 0) -> dict:
    key = jax.random.key(seed)
    keys = iter(jax.random.split(key, 40))
    n_a, n_b, n_c, n_d = (len(range(m, DEPTH, N_MIXERS)) for m in range(N_MIXERS))
    out_gain = (2.0 * DEPTH) ** -0.5

    def w(shape, fan_in, gain=1.0):
        return jax.random.normal(next(keys), shape, jnp.float32) * (gain * fan_in ** -0.5)

    def gain(shape):
        return 1.0 + 0.02 * jax.random.normal(next(keys), shape, jnp.float32)

    x = jax.random.normal(next(keys), (BATCH, SEQ, D_MODEL), jnp.float32)
    positions = jnp.broadcast_to(jnp.arange(SEQ, dtype=jnp.int32), (BATCH, SEQ))
    gla_in = 2 * GLA_KEY_DIM + 2 * GLA_VALUE_DIM + GLA_GATE_RANK
    return {
        "x": x,
        "positions": positions,
        "norm_mix": gain((DEPTH, D_MODEL)),
        "norm_ffn": gain((DEPTH, D_MODEL)),
        "hgrn_w_in": w((n_a, D_MODEL, 4 * D_MODEL), D_MODEL),
        "hgrn_g_norm": gain((n_a, HGRN_DV)),
        "hgrn_w_out": w((n_a, D_MODEL, D_MODEL), D_MODEL, out_gain),
        "hgrn_lb_logits": 0.5 * jax.random.normal(next(keys), (DEPTH + 1, D_MODEL), jnp.float32),
        "gla_w_in": w((n_b, D_MODEL, gla_in), D_MODEL),
        "gla_w_gk_up": w((n_b, GLA_GATE_RANK, GLA_KEY_DIM), GLA_GATE_RANK),
        "gla_b_gk": 0.01 * jax.random.normal(next(keys), (n_b, GLA_KEY_DIM), jnp.float32),
        "gla_g_norm": gain((n_b, GLA_DV)),
        "gla_w_out": w((n_b, GLA_VALUE_DIM, D_MODEL), GLA_VALUE_DIM, out_gain),
        "ret_w_in": w((n_c, D_MODEL, 6 * D_MODEL), D_MODEL),
        "ret_w_out": w((n_c, 2 * D_MODEL, D_MODEL), 2 * D_MODEL, out_gain),
        "mla_w_in": w((n_d, D_MODEL, MLA_Q_LORA + MLA_KV_LORA + MLA_ROPE), D_MODEL),
        "mla_g_q_lora": gain((n_d, MLA_Q_LORA)),
        "mla_g_kv_lora": gain((n_d, MLA_KV_LORA)),
        "mla_w_uq": w((n_d, MLA_Q_LORA, MLA_HEADS * MLA_QK), MLA_Q_LORA),
        "mla_w_ukv": w((n_d, MLA_KV_LORA, MLA_HEADS * (MLA_NOPE + MLA_V)), MLA_KV_LORA),
        "mla_g_qnorm": gain((n_d, MLA_QK)),
        "mla_g_knorm": gain((n_d, MLA_QK)),
        "mla_w_out": w((n_d, MLA_HEADS * MLA_V, D_MODEL), MLA_HEADS * MLA_V, out_gain),
        "ffn_w_gate_up": w((DEPTH, D_MODEL, 2 * FFN_HIDDEN), D_MODEL),
        "ffn_w_down": w((DEPTH, FFN_HIDDEN, D_MODEL), FFN_HIDDEN, out_gain),
    }

def reference(x, positions, norm_mix, norm_ffn,
              hgrn_w_in, hgrn_g_norm, hgrn_w_out, hgrn_lb_logits,
              gla_w_in, gla_w_gk_up, gla_b_gk, gla_g_norm, gla_w_out,
              ret_w_in, ret_w_out,
              mla_w_in, mla_g_q_lora, mla_g_kv_lora, mla_w_uq, mla_w_ukv,
              mla_g_qnorm, mla_g_knorm, mla_w_out,
              ffn_w_gate_up, ffn_w_down):
    lower_bounds = jnp.cumsum(jax.nn.softmax(hgrn_lb_logits.astype(jnp.float32), axis=0), axis=0)
    for i in range(DEPTH):
        mixer, j = i % N_MIXERS, i // N_MIXERS
        h = _rms_norm(x, norm_mix[i])
        if mixer == 0:
            y = _hgrn2(h, hgrn_w_in[j], hgrn_g_norm[j], hgrn_w_out[j], lower_bounds[i])
        elif mixer == 1:
            y = _gla(h, gla_w_in[j], gla_w_gk_up[j], gla_b_gk[j], gla_g_norm[j], gla_w_out[j])
        elif mixer == 2:
            y = _retnet(h, positions, ret_w_in[j], ret_w_out[j])
        else:
            y = _mla(h, positions, mla_w_in[j], mla_g_q_lora[j], mla_g_kv_lora[j], mla_w_uq[j],
                     mla_w_ukv[j], mla_g_qnorm[j], mla_g_knorm[j], mla_w_out[j])
        x = x + y.astype(x.dtype)
        h = _rms_norm(x, norm_ffn[i])
        x = x + _swiglu(h, ffn_w_gate_up[i], ffn_w_down[i]).astype(x.dtype)
    return x


_drawn_inputs = setup_inputs


def setup_inputs(seed=0):
    import zlib

    import numpy as np

    out = dict(_drawn_inputs(seed))
    spreads = {}
    factors = {'norm_mix': 3.608,
     'norm_ffn': 4.725,
     'hgrn_g_norm': 8.0,
     'hgrn_lb_logits': 4.118,
     'gla_b_gk': 33.093,
     'gla_g_norm': 32.334}
    for name, (base, spread) in spreads.items():
        noise = np.random.default_rng([zlib.crc32(name.encode()), seed]).standard_normal(out[name].shape)
        drawn = base * np.exp(spread * noise) if base else spread * noise
        out[name] = __import__('jax').numpy.asarray(drawn.astype(out[name].dtype))
    for name, factor in factors.items():
        out[name] = (out[name] * factor).astype(out[name].dtype)
    return out
```

```python
from contextlib import ExitStack

import concourse.bass as bass
from concourse import mybir

ALU = mybir.AluOpType
ACT = mybir.ActivationFunctionType
F32 = mybir.dt.float32
F32R = mybir.dt.float32r
U8 = mybir.dt.uint8

P = 128
EPS = 1e-6


class Tile:

    def __init__(self, c, m=0, i=0):
        self.c, self.m, self.i = c, m, i

    def plus(self, k):
        return Tile(self.c + k, self.m, self.i)

    def count(self, k):
        return self.c + k + (self.i * self.m if self.m else 0)

    def slot(self):
        return self.c % 2

    def landed(self):
        return 16 * (self.c // 2 + 1) + (self.i * (8 * self.m) if self.m else 0)


class NormSignals:

    def __init__(self, sem):
        self.sq = sem("xn_sq")
        self.stats = sem("xn_stats")
        self.hi = sem("xn_hi")
        self.lo = sem("xn_lo")
        self.ms = sem("xn_ms")
        self.rs = sem("xn_rs")
        self.dg = sem("xn_dg")
        self.bc = sem("xn_bc")
        self.ready = sem("xn_ready")


class MixerSignals:

    def __init__(self, sem, prefix):
        self.f_ready = sem(prefix + "f_ready")
        self.k_ready = sem(prefix + "k_ready")
        self.q_ready = sem(prefix + "q_ready")
        self.sig_f = sem(prefix + "sig_f")
        self.sig_q = sem(prefix + "sig_q")
        self.sig_g = sem(prefix + "sig_g")
        self.blocks = sem(prefix + "blocks")
        self.diag = sem(prefix + "diag")
        self.level = sem(prefix + "level")
        self.decayed = sem(prefix + "decayed")
        self.merged = sem(prefix + "merged")
        self.vt = sem(prefix + "vt")
        self.vn = sem(prefix + "vn")
        self.kt_t = sem(prefix + "kt_t")
        self.kt_c = sem(prefix + "kt_c")
        self.u = sem(prefix + "u")
        self.states = sem(prefix + "states")
        self.o_done = sem(prefix + "o_done")
        self.o_sq = sem(prefix + "o_sq")
        self.o_out = sem(prefix + "o_out")
        self.stats = sem(prefix + "stats")
        self.ms = sem(prefix + "ms")
        self.rs = sem(prefix + "rs")
        self.dg = sem(prefix + "dg")
        self.bc = sem(prefix + "bc")
        self.onorm = sem(prefix + "onorm")
        self.gs = sem(prefix + "gs")
        self.gated = sem(prefix + "gated")
        self.r_hi = sem(prefix + "r_hi")
        self.r_lo = sem(prefix + "r_lo")


class MlpSignals:

    def __init__(self, sem, prefix):
        self.sig = sem(prefix + "sig")
        self.gate = sem(prefix + "gate")
        self.hid = sem(prefix + "hid")
        self.r_hi = sem(prefix + "r_hi")
        self.r_lo = sem(prefix + "r_lo")


def trunk(nc, x, norm_mix, norm_ffn, hgrn_w_in, hgrn_g_norm, hgrn_w_out, hgrn_lb_logits,
          gla_w_in, gla_w_gk_up, gla_b_gk, gla_g_norm, gla_w_out, ffn_w_gate_up, ffn_w_down, out):
    T, D = x.shape[1], x.shape[2]
    DT = D // P
    NC = T // P
    HALF = T // 2
    HH = D // P
    GH = 4
    GK = GH * P
    RANK = gla_w_gk_up.shape[1]
    FH = ffn_w_down.shape[1]
    FT = FH // P
    GROUPS = [8, 8, FT - 16]
    LEVELS = 7
    STEPS = 1 + 2 * LEVELS
    SCALE = float(P) ** -0.5
    assert T == 1024 and DT == 8 and FT == 22 and NC == 8

    ctx = ExitStack()
    with ctx:
        base = (nc.sbuf_base + 63) // 64 * 64
        KB = 1024
        sizes = {}
        at = [base]

        def place(name, shape, dt=F32, offset=None):
            nbytes = 1
            for s in shape[1:]:
                nbytes *= s
            nbytes *= 1 if dt == U8 else 4
            if offset is None:
                offset = at[0]
                at[0] += (nbytes + 31) // 32 * 32
            return nc.alloc_sbuf_tensor_at(name, shape, dt, offset=offset)

        xT = place("xT", [P, DT, T])
        h_hi = place("h_hi", [P, DT, T], F32R)
        h_lo = place("h_lo", [P, DT, T], F32R)
        w_raw = place("w_raw", [P, 2, 8, P])
        w_hi = place("w_hi", [P, 2, 8, P], F32R)
        w_lo = place("w_lo", [P, 2, 8, P], F32R)
        rms_x = place("rms_x", [P, T])
        z = place("z", [P, 2, T])
        sg = place("sg", [P, T])
        aux = place("aux", [P, T])
        o_at = at[0]
        o = place("o", [P, DT, T])
        s_at = at[0]
        qp = place("qp", [P, T])
        ks = place("ks", [P, T])
        sc = place("sc", [P, NC, P])
        kt = place("kt", [P, T])
        fg = place("fg", [P, 2 * T])
        vn = place("vn", [P, 2 * T])
        r_lo = place("r_lo", [P, DT, T], F32R, o_at)
        r_hi = place("r_hi", [P, DT, T], F32R, s_at)
        ident = place("ident", [P, P])
        ones = place("ones", [P, P])
        cols = place("cols", [P, 64])
        mask = place("mask", [P, LEVELS, P // 2], U8)
        mhalf = place("mhalf", [P, NC])
        ms = place("ms", [P, NC])
        rs = place("rs", [P, NC])
        ssq = place("ssq", [P, NC])
        lbt = place("lbt", [P, 6, HH])
        nbg = place("nbg", [P, GH])
        rows = z[0:63, 0, 0:P]
        used = at[0] - base
        assert at[0] <= nc.sbuf_usable_end, (at[0], nc.sbuf_usable_end)
        arena = ctx.enter_context(nc.sbuf_tensor("arena", [P, used + 64], U8))
        MIX, FFN, LOGIT, HG, GG, BG = 0, 16, 32, 56, 57, 59

        pp = ctx.enter_context(nc.psum_tensor("pp", [P, 4, HALF], F32))
        pa = ctx.enter_context(nc.psum_tensor("pa", [P, 2, HALF], F32))
        pb = ctx.enter_context(nc.psum_tensor("pb", [P, 2, HALF], F32))

        def sem(name):
            return ctx.enter_context(nc.semaphore(name))

        landed = [sem("landed0"), sem("landed1")]
        hi_ready, lo_ready, tile_done, evac, asked = sem("hi_ready"), sem("lo_ready"), sem("tile_done"), sem("evac"), sem("asked")
        rows_in, x_in, up_in = sem("rows_in"), [sem(f"x_in{c}") for c in range(NC)], sem("up_in")
        const, cols_t, cols_ready, lb_step, lb_exp, nb_ready, mask_step = (sem("const"), sem("cols_t"), sem("cols_ready"),
                                                                 sem("lb_step"), sem("lb_exp"), sem("nb_ready"), sem("mask_step"))
        x_turned, x_stored, x_sq = sem("x_turned"), sem("x_stored"), sem("x_sq")
        xn = NormSignals(sem)
        out_t, out_c, out_done = sem("out_t"), sem("out_c"), [sem("out_done0"), sem("out_done1")]
        mh, mg = MixerSignals(sem, "h_"), MixerSignals(sem, "g_")
        zf, zs, f_part = sem("zf"), sem("zs"), sem("f_part")
        ff = [MlpSignals(sem, f"ff{l}_") for l in range(2)]

        def halves(ap):
            return ap.rearrange("p (k t) -> p k t", k=2)

        def tok(ap):
            return ap.rearrange("p (c t) -> p c t", c=NC)

        def pair(t):
            return pp[:, 2 * t.slot():2 * t.slot() + 2, :]

        def rms2():
            return halves(rms_x[:, :])

        def goff(j):
            return 2 * T - ((2 * T) >> j)

        sq = kt[:, :]
        dg = kt[:, :]
        g128 = fg[:, goff(7):goff(7) + NC]
        stH = fg[:, 0:7 * P].rearrange("p (c v) -> p c v", c=7)
        stG = fg[:, 0:7 * 2 * P].rearrange("p (c v) -> p c v", c=7)
        vnH = vn[:, 0:NC * P].rearrange("p (c v) -> p c v", c=NC)
        vnG = vn[:, :].rearrange("p (c v) -> p c v", c=NC)
        ktc = tok(kt[:, :])

        def wcols(w, k0, n, col, width=P):
            return w[k0 * P:(k0 + n) * P, bass.ds(col, width)].rearrange("(k p) c -> p k c", p=P)

        W_H, W_G = hgrn_w_in[0], gla_w_in[0]
        N_H = 0
        N_HO = N_H + 4 * HH
        N_F0 = N_HO + DT
        FFN_TILES = 2 * FT + 3 * DT
        N_GK = N_F0 + FFN_TILES
        N_G = N_GK + 1
        N_GO = N_G + 6 * GH
        N_F1 = N_GO + DT
        N_END = N_F1 + FFN_TILES

        def ffn_starts(n0):
            res, n, f0 = [], n0, 0
            for g, k in enumerate(GROUPS):
                res.append((f0, k, n, n + 2 * k, g == len(GROUPS) - 1))
                n += 2 * k + DT
                f0 += k
            return res

        block = ctx.enter_context(nc.Block())

        @block.sync
        def _(sp):
            for at_row, src in ((MIX, norm_mix.rearrange("l (t p) -> (l t) p", p=P)),
                                (FFN, norm_ffn.rearrange("l (t p) -> (l t) p", p=P)),
                                (LOGIT, hgrn_lb_logits.rearrange("l (t p) -> (l t) p", p=P)),
                                (HG, hgrn_g_norm), (GG, gla_g_norm.rearrange("l (t p) -> (l t) p", p=P)),
                                (BG, gla_b_gk.rearrange("l (t p) -> (l t) p", p=P))):
                sp.dma_start(z[at_row:at_row + src.shape[0], 0, 0:P], src).then_inc(rows_in, 16)

            def load(t, w, col, k0=0, n=8, width=P):
                if not (t.m == 0 and t.c < 2):
                    sp.wait_ge(lo_ready, t.count(-1))
                    sp.sem_inc(asked, 1)
                sp.dma_start(w_raw[:, t.slot(), 0:n, 0:width],
                             wcols(w, k0, n, col, width)).then_inc(landed[t.slot()], 16)

            xv = x.rearrange("b (c p) d -> (b c) p d", p=P)
            for c in range(NC):
                sp.dma_start(o[:, c, :], xv[c]).then_inc(x_in[c], 16)

            def hgrn_loads(t, h):
                load(t, W_H, h * P + D)
                load(t.plus(1), W_H, h * P)
                load(t.plus(2), W_H, h * P + 2 * D)

            def mlp_loads(n0, l):
                for f0, k, n, nd, _ in ffn_starts(n0):
                    with sp.Fori(0, k) as i:
                        load(Tile(n, 2, i), ffn_w_gate_up[l], i * P + f0 * P)
                        load(Tile(n + 1, 2, i), ffn_w_gate_up[l], i * P + (f0 * P + FH))
                    with sp.Fori(0, DT // 2) as i:
                        load(Tile(nd, 2, i), ffn_w_down[l], i * (2 * P), f0, k)
                        load(Tile(nd + 1, 2, i), ffn_w_down[l], i * (2 * P) + P, f0, k)

            hgrn_loads(Tile(N_H), 0)
            with sp.Fori(1, HH) as h:
                hgrn_loads(Tile(N_H - 1, 4, h), h)
                load(Tile(N_H + 2, 4, h), W_H, h * P + (3 * D - P))
            load(Tile(N_HO - 1), W_H, 4 * D - P)
            with sp.Fori(0, DT // 2) as i:
                load(Tile(N_HO, 2, i), hgrn_w_out[0], i * (2 * P))
                load(Tile(N_HO + 1, 2, i), hgrn_w_out[0], i * (2 * P) + P)
            mlp_loads(N_F0, 0)

            load(Tile(N_GK), W_G, 2 * GK + 2 * D, width=RANK)
            sp.wait_ge(tile_done, N_GK)
            sp.dma_start(o[0:RANK, 0, 0:GK], gla_w_gk_up[0]).then_inc(up_in, 16)

            def gla_loads(t, h):
                load(t, W_G, h * (2 * P) + 2 * GK)
                load(t.plus(1), W_G, h * (2 * P) + (2 * GK + P))
                load(t.plus(2), W_G, h * P)
                load(t.plus(3), W_G, h * P + GK)

            gla_loads(Tile(N_G), 0)
            with sp.Fori(1, GH) as h:
                gla_loads(Tile(N_G - 2, 6, h), h)
                load(Tile(N_G + 2, 6, h), W_G, h * (2 * P) + (2 * GK + D - 2 * P))
                load(Tile(N_G + 3, 6, h), W_G, h * (2 * P) + (2 * GK + D - P))
            load(Tile(N_GO - 2), W_G, 2 * GK + 2 * D - 2 * P)
            load(Tile(N_GO - 1), W_G, 2 * GK + 2 * D - P)
            with sp.Fori(0, DT // 2) as i:
                load(Tile(N_GO, 2, i), gla_w_out[0], i * (2 * P))
                load(Tile(N_GO + 1, 2, i), gla_w_out[0], i * (2 * P) + P)
            mlp_loads(N_F1, 1)

        @block.tensor
        def _(pe):
            def tile(t, hi, lo, n=8, slots=None, ready=None, order=None):
                slots = slots or {}
                pe.wait_ge(lo_ready, t.count(1))
                if not (t.m == 0 and t.c < 2):
                    pe.wait_ge(evac, t.count(-1))
                order = order or list(range(n))
                s = t.slot()
                for at_k, k in enumerate(order):
                    if ready:
                        ready(k, at_k)
                    first, last = at_k == 0, at_k == n - 1
                    for w, act, st, sp_ in ((w_hi, hi, first, False), (w_hi, lo, False, False),
                                            (w_lo, hi, False, last)):
                        for half in range(2):
                            mm = pe.matmul(pp[:, 2 * s + half, :], w[:, s, k, :],
                                           act[:, k, half * HALF:(half + 1) * HALF], start=st, stop=sp_)
                    if last:
                        mm.then_inc(tile_done, 1)
                    for emit in slots.get(at_k, ()):
                        emit()

            def diagonal(m, h):
                if m is mh:
                    pe.wait_ge(mh.k_ready, h + 1)
                    pe.wait_ge(mh.q_ready, h + 1)
                else:
                    pe.wait_ge(evac, N_G + 4 if isinstance(h, int) and h == 0 else h * 6 + (N_G + 2))
                if not isinstance(h, int) or h > 0:
                    pe.wait_ge(m.states, h * 7)
                    pe.wait_ge(m.ms, h)
                for c in range(NC):
                    mm = pe.matmul(pa[:, c // 4, (c % 4) * P:(c % 4 + 1) * P], ks[:, c * P:(c + 1) * P],
                                   qp[:, c * P:(c + 1) * P], start=True, stop=True)
                mm.then_inc(m.diag, 1)

            def level(m, h, j):
                b = 1 << j
                pe.wait_ge(m.decayed, h * STEPS + (1 + 2 * j))
                pe.wait_ge(m.merged, h * 8 + max(1, j))
                qv = qp[:, :].rearrange("p (c k s) -> p c k s", c=NC, s=2 * b)[:, :, :, b:]
                for c in range(NC):
                    mm = pe.matmul(pa[:, j % 2, c * 64:(c + 1) * 64].rearrange("p (k s) -> p k s", s=b),
                                   ks[:, c * P:(c + 1) * P], qv[:, c], start=True, stop=True)
                mm.then_inc(m.level, 1)

            def turn_keys(m, h):
                pe.wait_ge(m.decayed, h * STEPS + STEPS)
                for bank in (1, 0):
                    pe.wait_ge(m.merged, h * 8 + (7 if bank else 8))
                    if bank == 1 and m is mh:
                        pe.wait_ge(m.vn, h * 2 + 1)
                    if bank == 0 and m is mh:
                        pe.wait_ge(m.vn, h * 2 + 2)
                    for c in range(4 * bank, 4 * bank + 4):
                        mm = pe.transpose(pa[:, bank, (c % 4) * P:(c % 4 + 1) * P],
                                          ks[:, c * P:(c + 1) * P], ident[:, :])
                    mm.then_inc(m.kt_t, 1)

            def updates(h):
                pe.wait_ge(mh.kt_c, h * 2 + 2)
                for bank in (1, 0):
                    cs = range(4, 7) if bank else range(0, 4)
                    for c in cs:
                        mm = pe.matmul(pa[:, bank, (c % 4) * P:(c % 4 + 1) * P], ktc[:, c, :], vnH[:, c, :],
                                       start=True, stop=True)
                    mm.then_inc(mh.u, 1)

            def updates_g(h, part):
                pe.wait_ge(mg.kt_c, h * 2 + 2)
                for q in range(2):
                    if part:
                        pe.wait_ge(mg.states, h * 7 + 2 * (q + 1))
                    for c in (4 * part + 2 * q, 4 * part + 2 * q + 1):
                        if c < 7:
                            mm = pe.matmul(pa[:, 1 - q, (c % 2) * 256:(c % 2 + 1) * 256], ktc[:, c, :],
                                           vnG[:, c, :], start=True, stop=True)
                    mm.then_inc(mg.u, 1)

            def intra(m, h, val, first_wait=True):
                pe.wait_ge(m.merged, h * 8 + 8)
                for c in range(NC):
                    pe.matmul(pb[:, c // 4, (c % 4) * P:(c % 4 + 1) * P], val(c), sc[:, c, :],
                              start=(c % 4 == 0), stop=(c == 0), skip_group_check=True)

            def inter(m, h, st):
                pe.wait_ge(m.states, h * 7 + 7)
                for c in range(1, NC):
                    mm = pe.matmul(pb[:, c // 4, (c % 4) * P:(c % 4 + 1) * P], st(c - 1), qp[:, c * P:(c + 1) * P],
                                   start=False, stop=True, skip_group_check=True)
                mm.then_inc(m.o_done, 1)

            def stats_of(ps, src, start, done):
                for c in range(NC):
                    mm = pe.matmul(ps[:, c:c + 1], src[:, c * P:(c + 1) * P], ones[:, 0:1],
                                   start=(start and c == 0), stop=True, skip_group_check=True)
                mm.then_inc(done, 1)

            def spread(src, done):
                for half in range(2):
                    mm = pe.matmul(pb[:, half, :], ones[:, :], src[:, half * HALF:(half + 1) * HALF],
                                   start=True, stop=True)
                mm.then_inc(done, 1)

            pe.wait_ge(const, 2)
            pe.wait_ge(rows_in, 96)
            pe.transpose(pp[:, 0, 0:63], rows, ident[0:63, 0:63]).then_inc(cols_t, 1)
            for c in range(NC):
                pe.wait_ge(x_in[c], 16)
                ps = pb if c % 2 else pa
                if c >= 2:
                    pe.wait_ge(x_stored, c - 1)
                for d in range(DT):
                    mm = pe.transpose(ps[:, d // 4, (d % 4) * P:(d % 4 + 1) * P], o[:, c, d * P:(d + 1) * P],
                                      ident[:, :])
                mm.then_inc(x_turned, 1)
            pe.wait_ge(cols_ready, 1)

            def h_ready(norm):
                def ready(k, at_k):
                    pe.wait_ge(xn.lo, DT * norm + k + 1)
                return ready

            def x_stats(d_count, start):
                def emit():
                    pe.wait_ge(xn.sq, d_count)
                    stats_of(pa[:, 1, :], aux[:, :], start, xn.stats)
                return emit

            def x_spread(norm):
                def emit():
                    pe.wait_ge(xn.dg, norm + 1)
                    spread(aux[:, :], xn.bc)
                return emit

            def turn_values(h):
                for bank in (1, 0):
                    pe.wait_ge(mh.merged, h * 8 + (7 if bank else 8))
                    if bank == 1:
                        pe.wait_ge(evac, zi_count(h))
                    for c in range(4 * bank, 4 * bank + 4):
                        mm = pe.transpose(pa[:, bank, (c % 4) * P:(c % 4 + 1) * P], z[:, 0, c * P:(c + 1) * P],
                                          ident[:, :])
                    mm.then_inc(mh.vt, 1)

            def zi_count(h):
                return 3 if isinstance(h, int) and h == 0 else h * 4 + 2

            def h_intra(h, later):
                if later:
                    pe.wait_ge(mh.onorm, h)
                else:
                    pe.wait_ge(xn.ready, 1)
                intra(mh, h, lambda c: vnH[:, c, :])

            def h_stats(h):
                pe.wait_ge(mh.o_sq, h + 1)
                stats_of(pa[:, 1, :], sq, True, mh.stats)

            def h_spread(h):
                pe.wait_ge(mh.dg, h + 1)
                pe.wait_ge(mh.o_out, h + 1)
                spread(dg, mh.bc)

            def hgrn(t, h, later):
                p = h - 1
                tile(t, h_hi, h_lo, slots={
                    1: [lambda: level(mh, p, 6)], 3: [lambda: turn_values(p)],
                    5: [lambda: turn_keys(mh, p)], 7: [lambda: updates(p)]})
                tile(t.plus(1), h_hi, h_lo, slots={
                    1: [lambda: h_intra(p, later)], 3: [lambda: inter(mh, p, lambda c: stH[:, c, :])],
                    7: [lambda: h_stats(p)]})
                tile(t.plus(2), h_hi, h_lo, slots={
                    3: [lambda: h_spread(p), lambda: diagonal(mh, h)],
                    5: [lambda: level(mh, h, 0)], 7: [lambda: level(mh, h, 1)]})
                tile(t.plus(3), h_hi, h_lo, slots={
                    1: [lambda: level(mh, h, 2)], 3: [lambda: level(mh, h, 3)],
                    5: [lambda: level(mh, h, 4)], 7: [lambda: level(mh, h, 5)]})

            x_spread(0)()
            hgrn_first = Tile(N_H)
            tile(hgrn_first, h_hi, h_lo, ready=h_ready(0))
            tile(hgrn_first.plus(1), h_hi, h_lo)
            tile(hgrn_first.plus(2), h_hi, h_lo, slots={3: [lambda: diagonal(mh, 0)],
                                                        5: [lambda: level(mh, 0, 0)], 7: [lambda: level(mh, 0, 1)]})
            for j in range(2, 6):
                level(mh, 0, j)
            hgrn(Tile(N_H + 3), 1, False)
            with pe.Fori(2, HH) as h:
                hgrn(Tile(N_H - 1, 4, h), h, True)
            last = HH - 1
            tile(Tile(N_HO - 1), h_hi, h_lo, slots={
                1: [lambda: level(mh, last, 6)], 3: [lambda: turn_values(last)],
                5: [lambda: turn_keys(mh, last)], 7: [lambda: updates(last)]})
            h_intra(last, True)
            inter(mh, last, lambda c: stH[:, c, :])

            def to_x(n0, n, ready, order=None, first_slots=None, norm=None, final=False):
                def slot(d_done, start, par):
                    if norm is not None:
                        return {3: [x_stats(d_done, start)]}
                    if final:
                        return {3: [turn_out(d_done, par)]}
                    return {}

                base_d = DT * (norm - 1) if norm is not None else 0
                tile(Tile(n0), r_hi, r_lo, n, slots=first_slots, ready=ready, order=order)
                tile(Tile(n0 + 1), r_hi, r_lo, n, slots=slot(base_d + 1, True, 0))
                with pe.Fori(1, DT // 2) as i:
                    tile(Tile(n0, 2, i), r_hi, r_lo, n, slots=slot(i * 2 + base_d, False, 1))
                    tile(Tile(n0 + 1, 2, i), r_hi, r_lo, n, slots=slot(i * 2 + (base_d + 1), False, 0))

            def turn_out(d_done, par):
                def emit():
                    first = isinstance(d_done, int) and d_done == 1
                    pe.wait_ge(evac, d_done + (N_END - DT))
                    if not first:
                        pe.wait_ge(out_c, d_done - 1)
                    for c in range(NC):
                        mm = pe.transpose(pa[:, c // 4, (c % 4) * P:(c % 4 + 1) * P],
                                          z[:, par, c * P:(c + 1) * P], ident[:, :])
                    mm.then_inc(out_t, 1)
                return emit

            def split_ready(m, order):
                def ready(k, at_k):
                    pe.wait_ge(m.r_lo, at_k + 1)
                return ready

            order_h = [0, 1, 2, 4, 5, 6, 3, 7]
            to_x(N_HO, 8, split_ready(mh, order_h), order_h,
                 {1: [lambda: h_stats(last)], 5: [lambda: h_spread(last)]}, norm=1)

            def mlp(l, n0, norm):
                for f0, k, n, nd, end in ffn_starts(n0):
                    lead = 1 if f0 == 0 else 0
                    if lead:
                        tile(Tile(n), h_hi, h_lo, ready=h_ready(norm),
                             slots={1: [x_stats(DT * norm, False)], 5: [x_spread(norm)]})
                        tile(Tile(n + 1), h_hi, h_lo)
                    with pe.Fori(lead, k) as i:
                        tile(Tile(n, 2, i), h_hi, h_lo)
                        tile(Tile(n + 1, 2, i), h_hi, h_lo)

                    def hid_ready(kk, at_k, f0=f0):
                        pe.wait_ge(ff[l].r_lo, f0 + kk + 1)
                    to_x(nd, k, hid_ready, norm=norm + 1 if end and l == 0 else None, final=end and l == 1)

            mlp(0, N_F0, 1)

            def z_gate(h):
                def emit():
                    ps = pb if h % 2 else pa
                    if h == 0:
                        pe.wait_ge(up_in, 16)
                        pe.wait_ge(evac, N_GK + 1)
                        pe.wait_ge(xn.ms, 3)
                    if h == 1:
                        pe.wait_ge(xn.ready, 3)
                    if h >= 2:
                        pe.wait_ge(zs, 5 * (h - 1))
                    for half in range(2):
                        mm = pe.matmul(ps[:, half, :], o[0:RANK, 0, h * P:(h + 1) * P],
                                       aux[0:RANK, half * HALF:(half + 1) * HALF], start=True, stop=True)
                    mm.then_inc(zf, 1)
                return emit

            def g_turn_values(h, j):
                for bank in (0, 1):
                    if j == 0:
                        pe.wait_ge(evac, N_G + 1 if isinstance(h, int) and h == 0 else h * 6 + (N_G - 1))
                        if not (isinstance(h, int) and h == 0):
                            pe.wait_ge(mg.states, h * 7)
                            pe.wait_ge(mg.ms, h)
                    else:
                        pe.wait_ge(evac, N_G + 2 if isinstance(h, int) and h == 0 else h * 6 + N_G)
                        pe.wait_ge(mg.vn, h * 4 + bank + 1)
                    for c in range(4 * bank, 4 * bank + 4):
                        mm = pe.transpose(pa[:, bank, (c % 4) * P:(c % 4 + 1) * P], z[:, j, c * P:(c + 1) * P],
                                          ident[:, :])
                    mm.then_inc(mg.vt, 1)

            def g_diag(h):
                pe.wait_ge(mg.vn, h * 4 + 4)
                diagonal(mg, h)

            def g_intra(h, j, later=True):
                if j == 0 and later:
                    pe.wait_ge(mg.onorm, h * 2)
                elif j == 0:
                    pe.wait_ge(zs, 5 * GH)
                if j == 1:
                    pe.wait_ge(mg.o_out, h * 2 + 1)
                intra(mg, h, lambda c: vnG[:, c, j * P:(j + 1) * P])

            def g_inter(h, j):
                inter(mg, h, lambda c: stG[:, c, j * P:(j + 1) * P])

            def g_stats(h, j):
                pe.wait_ge(mg.o_sq, h * 2 + j + 1)
                stats_of(pa[:, 1, :], sq, j == 0, mg.stats)

            def g_spread(h):
                pe.wait_ge(mg.dg, h + 1)
                pe.wait_ge(mg.o_out, h * 2 + 2)
                spread(dg, mg.bc)

            def g_levels(h):
                return ({1: [lambda: g_diag(h)], 3: [lambda: level(mg, h, 0)],
                         5: [lambda: level(mg, h, 1)], 7: [lambda: level(mg, h, 2)]},
                        {1: [lambda: level(mg, h, 3)], 3: [lambda: level(mg, h, 4)],
                         5: [lambda: level(mg, h, 5)], 7: [lambda: level(mg, h, 6)]})

            def gla(t, h, later):
                p = h - 1
                tile(t, h_hi, h_lo, slots={1: [lambda: turn_keys(mg, p)], 3: [lambda: updates_g(p, 0)],
                                           5: [lambda: updates_g(p, 1)], 7: [lambda: g_intra(p, 0, later)]})
                tile(t.plus(1), h_hi, h_lo, slots={1: [lambda: g_inter(p, 0)], 5: [lambda: g_stats(p, 0)],
                                                   7: [lambda: g_intra(p, 1), lambda: g_inter(p, 1)]})
                tile(t.plus(2), h_hi, h_lo, slots={3: [lambda: g_stats(p, 1)], 7: [lambda: g_turn_values(h, 0)]})
                tile(t.plus(3), h_hi, h_lo, slots={1: [lambda: g_spread(p)], 3: [lambda: g_turn_values(h, 1)]})
                a, b = g_levels(h)
                tile(t.plus(4), h_hi, h_lo, slots=a)
                tile(t.plus(5), h_hi, h_lo, slots=b)

            tile(Tile(N_GK), h_hi, h_lo, ready=h_ready(2), slots={1: [x_stats(DT * 2, False)], 5: [x_spread(2)]})
            tile(Tile(N_G), h_hi, h_lo, slots={3: [z_gate(0)], 7: [z_gate(1)]})
            tile(Tile(N_G + 1), h_hi, h_lo, slots={7: [z_gate(2)]})
            tile(Tile(N_G + 2), h_hi, h_lo, slots={7: [z_gate(3)]})

            def first_values(j):
                if j == 0:
                    pe.wait_ge(zs, 15)
                g_turn_values(0, j)
            tile(Tile(N_G + 3), h_hi, h_lo, slots={5: [lambda: first_values(0)], 7: [lambda: first_values(1)]})
            a, b = g_levels(0)
            for part in (a, b):
                for k in (1, 3, 5, 7):
                    for emit in part[k]:
                        emit()
            gla(Tile(N_G + 4), 1, False)
            with pe.Fori(2, GH) as h:
                gla(Tile(N_G - 2, 6, h), h, True)
            lastg = GH - 1
            tile(Tile(N_GO - 2), h_hi, h_lo, slots={
                1: [lambda: turn_keys(mg, lastg)], 3: [lambda: updates_g(lastg, 0)],
                5: [lambda: updates_g(lastg, 1)], 7: [lambda: g_intra(lastg, 0)]})
            tile(Tile(N_GO - 1), h_hi, h_lo, slots={
                1: [lambda: g_inter(lastg, 0)], 5: [lambda: g_stats(lastg, 0)],
                7: [lambda: g_intra(lastg, 1), lambda: g_inter(lastg, 1)]})
            order_g = [0, 1, 2, 4, 5, 3, 6, 7]
            to_x(N_GO, 8, split_ready(mg, order_g), order_g,
                 {1: [lambda: g_stats(lastg, 1)], 4: [lambda: g_spread(lastg)]}, norm=3)
            mlp(1, N_F1, 3)
            turn_out(DT, 1)()

        @block.scalar
        def _(act):
            def split(t):
                act.wait_ge(landed[t.slot()], t.landed())
                if not (t.m == 0 and t.c < 2):
                    act.wait_ge(tile_done, t.count(-1))
                act.activation(w_hi[:, t.slot(), :, :], w_raw[:, t.slot(), :, :], ACT.Copy).then_inc(hi_ready, 1)

            def step(t):
                split(t.plus(2))

            act.wait_ge(cols_t, 1)
            act.activation(cols[:, 0:63], pp[:, 0, 0:63], ACT.Copy).then_inc(cols_ready, 1)
            act.wait_ge(lb_step, 3)
            act.activation(lbt[:, 0:3, :], lbt[:, 0:3, :], ACT.Exp).then_inc(lb_exp, 1)
            for c in range(NC):
                act.wait_ge(x_in[c], 16)
                if c:
                    act.wait_ge(x_sq, c)
                act.activation(sg[:, :], o[:, c, :], ACT.Square, accum_out=ssq[:, c:c + 1]).then_inc(x_sq, 1)

            def gain_split(xs, col, hi):
                return act.activation(hi, xs, ACT.Copy, scale=col)

            for k in range(2):
                act.wait_ge(landed[k], 16)
                act.activation(w_hi[:, k, :, :], w_raw[:, k, :, :], ACT.Copy).then_inc(hi_ready, 1)
            act.wait_ge(cols_ready, 1)
            act.wait_ge(x_stored, NC)
            for d in range(DT):
                gain_split(xT[:, d, :], cols[:, MIX + d:MIX + d + 1], h_hi[:, d, :]).then_inc(xn.hi, 1)

            def store_rms(norm):
                act.wait_ge(xn.bc, norm + 1)
                if norm:
                    act.wait_ge(evac, {1: N_F0, 2: N_GK, 3: N_F1}[norm])
                act.activation(rms2(), pb[:, :, :], ACT.Copy).then_inc(xn.ready, 1)

            store_rms(0)

            def keys_copy(m, h, first):
                if not first:
                    act.wait_ge(m.bc, h)
                for q, bank in enumerate((1, 0)):
                    act.wait_ge(m.kt_t, h * 2 + q + 1)
                    act.activation(kt[:, bank * HALF:(bank + 1) * HALF], pa[:, bank, :], ACT.Copy).then_inc(m.kt_c, 1)

            def values_copy(h, first):
                if not first:
                    act.wait_ge(mh.o_done, h)
                for q, bank in enumerate((1, 0)):
                    act.wait_ge(mh.vt, h * 2 + q + 1)
                    act.activation(vnH[:, 4 * bank:4 * bank + 4, :],
                                   pa[:, bank, :].rearrange("p (c v) -> p c v", c=4), ACT.Copy).then_inc(mh.vn, 1)

            def out_copy(m, n_done, o_tile, col, sq_wait=None):
                act.wait_ge(m.o_done, n_done)
                if sq_wait:
                    act.wait_ge(*sq_wait)
                act.activation(halves(sq), pb[:, :, :], ACT.Square).then_inc(m.o_sq, 1)
                act.activation(halves(o_tile), pb[:, :, :], ACT.Copy, scale=col).then_inc(m.o_out, 1)

            def o_tile(k):
                return o[:, bass.ds(k, 1), :].rearrange("p a t -> p (a t)") if not isinstance(k, int) else o[:, k, :]

            def sigmoid(t, slot, done):
                act.wait_ge(evac, t.count(1))
                act.activation(sg[:, :], z[:, slot, :], ACT.Sigmoid).then_inc(done, 1)

            def hgrn(t, h, first, gate=True):
                p = h - 1
                if not first:
                    values_copy(p, isinstance(h, int) and h == 1)
                    keys_copy(mh, p, isinstance(h, int) and h == 1)
                step(t)
                if not first:
                    act.wait_ge(mh.q_ready, h)
                    act.wait_ge(mh.gated, h)
                sigmoid(t, 0, mh.sig_f)
                if not first:
                    out_copy(mh, h, o_tile(p), cols[:, HG:HG + 1])
                step(t.plus(1))
                act.wait_ge(mh.f_ready, h + 1)
                sigmoid(t.plus(1), 1, mh.sig_q)
                step(t.plus(2))
                if not first:
                    step(t.plus(3))
                    act.wait_ge(mh.q_ready, h + 1)
                    sigmoid(t.plus(3), 1, mh.sig_g)

            hgrn(Tile(N_H), 0, True)
            hgrn(Tile(N_H + 3), 1, False)
            with act.Fori(2, HH) as h:
                hgrn(Tile(N_H - 1, 4, h), h, False)
            last = HH - 1
            values_copy(last, False)
            keys_copy(mh, last, False)
            step(Tile(N_HO - 1))
            act.wait_ge(mh.gated, HH)
            sigmoid(Tile(N_HO - 1), 1, mh.sig_g)
            out_copy(mh, HH, o[:, last, :], cols[:, HG:HG + 1])

            def split_out(m, order, waits):
                for k in order:
                    for w in waits.get(k, ()):
                        act.wait_ge(*w)
                    act.activation(r_hi[:, k, :], o[:, k, :], ACT.Copy).then_inc(m.r_hi, 1)

            def to_x(n0, norm=None, final=False, skip_last=False):
                def one(t, d):
                    step_t = not (final and t.m == 0 and t.c + 2 >= N_END)
                    if step_t:
                        step(t)
                    if norm is not None:
                        gains = MIX + DT if norm == 2 else FFN + DT * (norm // 2)
                        xs = xT[:, d, :] if isinstance(d, int) else xT[:, bass.ds(d, 1), :].rearrange("p a t -> p (a t)")
                        hi = h_hi[:, d, :] if isinstance(d, int) else h_hi[:, bass.ds(d, 1), :].rearrange("p a t -> p (a t)")
                        if not (isinstance(d, int) and d == 0):
                            act.wait_ge(xn.stats, d + DT * (norm - 1))
                        act.wait_ge(evac, t.count(1))
                        act.activation(hi, xs, ACT.Copy, scale=cols[:, bass.ds(d + gains, 1)]).then_inc(xn.hi, 1)
                        act.activation(aux[:, :], xs, ACT.Square).then_inc(xn.sq, 1)
                    if final:
                        par = t.slot() ^ (n0 % 2)
                        act.wait_ge(out_t, d + 1)
                        if not (isinstance(d, int) and d < 2):
                            act.wait_ge(out_done[par], (d - par) * 8)
                        stage = (sg if par == 0 else aux)[:, :]
                        act.activation(halves(stage), pa[:, :, :], ACT.Copy).then_inc(out_c, 1)
                        act.wait_ge(out_c, d + 1)
                        dst = out[0].rearrange("(c p) d -> p c d", p=P)[:, :, bass.ds(d * P, P)]
                        act.dma_start(dst, tok(stage)).then_inc(out_done[par], 16)

                if final:
                    one(Tile(n0), 0)
                    one(Tile(n0 + 1), 1)
                    with act.Fori(1, DT // 2 - 1) as i:
                        one(Tile(n0, 2, i), i * 2)
                        one(Tile(n0 + 1, 2, i), i * 2 + 1)
                    one(Tile(n0 + DT - 2), DT - 2)
                    one(Tile(n0 + DT - 1), DT - 1)
                else:
                    one(Tile(n0), 0)
                    one(Tile(n0 + 1), 1)
                    with act.Fori(1, DT // 2) as i:
                        one(Tile(n0, 2, i), i * 2)
                        one(Tile(n0 + 1, 2, i), i * 2 + 1)

            split_out(mh, [0, 1, 2, 4, 5, 6, 3, 7], {0: [(mh.gated, HH)], 3: [(mh.bc, HH)], 7: [(mh.gated, HH + 1)]})
            to_x(N_HO, norm=1)

            def mlp(l, n0, norm):
                for f0, k, n, nd, end in ffn_starts(n0):
                    def pair_(t, i, f0=f0):
                        step(t)
                        act.wait_ge(evac, t.count(1))
                        act.activation(sg[:, :], z[:, 0, :], ACT.Sigmoid).then_inc(ff[l].sig, 1)
                        step(t.plus(1))
                        act.wait_ge(ff[l].hid, i + (f0 + 1))
                        dst = r_hi[:, i, :] if isinstance(i, int) else r_hi[:, bass.ds(i, 1), :].rearrange("p a t -> p (a t)")
                        act.activation(dst, z[:, 0, :], ACT.Copy).then_inc(ff[l].r_hi, 1)
                    lead = 1 if f0 == 0 else 0
                    if lead:
                        store_rms(norm)
                        pair_(Tile(n), 0)
                    with act.Fori(lead, k) as i:
                        pair_(Tile(n, 2, i), i)
                    to_x(nd, norm=norm + 1 if end and l == 0 else None, final=end and l == 1)

            mlp(0, N_F0, 1)

            def gate_parts(h):
                ps = (pb if h % 2 else pa)[:, :, :]
                act.wait_ge(zf, h + 1)
                if h:
                    act.wait_ge(f_part, h)
                f = o[:, 4 + h, :]
                act.activation(halves(sg[:, :]), ps, ACT.Abs, bias=cols[:, BG + h:BG + h + 1]).then_inc(zs, 1)
                act.wait_ge(zs, 5 * h + 1)
                act.activation(sg[:, :], sg[:, :], ACT.Exp, scale=-1.0).then_inc(zs, 1)
                act.wait_ge(zs, 5 * h + 2)
                act.activation(sg[:, :], sg[:, :], ACT.Ln, bias=1.0).then_inc(zs, 1)
                act.wait_ge(zs, 5 * h + 3)
                act.activation(f, sg[:, :], ACT.Exp, scale=-1.0 / 16).then_inc(zs, 1)
                act.wait_ge(zs, 5 * h + 4)
                act.activation(halves(sg[:, :]), ps, ACT.Relu, scale=-1.0, bias=nbg[:, h:h + 1]).then_inc(zs, 1)
                act.wait_ge(zs, 5 * h + 5)
                act.activation(sg[:, :], sg[:, :], ACT.Exp, scale=-1.0 / 16).then_inc(mg.sig_f, 1)

            store_rms(2)
            act.wait_ge(nb_ready, 1)
            step(Tile(N_GK))
            step(Tile(N_G))
            gate_parts(0)
            step(Tile(N_G + 1))
            gate_parts(1)
            gate_parts(2)
            step(Tile(N_G + 2))
            gate_parts(3)
            act.wait_ge(f_part, GH)

            def g_values_copy(h, j):
                for bank in (0, 1):
                    act.wait_ge(mg.vt, h * 4 + 2 * j + bank + 1)
                    act.activation(vnG[:, 4 * bank:4 * bank + 4, j * P:(j + 1) * P],
                                   pa[:, bank, :].rearrange("p (c v) -> p c v", c=4), ACT.Copy).then_inc(mg.vn, 1)

            step(Tile(N_G + 3))
            g_values_copy(0, 0)
            g_values_copy(0, 1)

            def g_out(h, j):
                out_copy(mg, h * 2 + j + 1, o_tile(h * 2 + j), cols[:, GG + j:GG + j + 1],
                         (mg.stats, h * 2 + 1) if j else None)

            def g_gate(t, p, j):
                if j:
                    act.wait_ge(mg.gated, p * 2 + 2)
                sigmoid(t, j, mg.sig_g)

            def gla(t, h):
                p = h - 1
                keys_copy(mg, p, isinstance(h, int) and h == 1)
                step(t)
                g_out(p, 0)
                step(t.plus(1))
                g_out(p, 1)
                step(t.plus(2))
                g_values_copy(h, 0)
                g_values_copy(h, 1)
                step(t.plus(3))
                step(t.plus(4))
                if not (isinstance(h, int) and h == 1):
                    act.wait_ge(mg.gated, p * 2 + 1)
                g_gate(t.plus(4), p, 0)
                step(t.plus(5))
                g_gate(t.plus(5), p, 1)

            gla(Tile(N_G + 4), 1)
            with act.Fori(2, GH) as h:
                gla(Tile(N_G - 2, 6, h), h)
            keys_copy(mg, GH - 1, False)
            step(Tile(N_GO - 2))
            act.wait_ge(mg.gated, 2 * GH - 1)
            sigmoid(Tile(N_GO - 2), 0, mg.sig_g)
            g_out(GH - 1, 0)
            step(Tile(N_GO - 1))
            g_out(GH - 1, 1)
            split_out(mg, [0, 1, 2, 4, 5], {0: [(mg.gated, 2 * GH - 1)]})
            act.wait_ge(mg.gated, 2 * GH)
            sigmoid(Tile(N_GO - 1), 1, mg.sig_g)
            split_out(mg, [3, 6, 7], {3: [(mg.bc, GH)], 6: [(mg.gated, 2 * GH)], 7: [(mg.gated, 2 * GH + 1)]})
            to_x(N_GO, norm=3)
            mlp(1, N_F1, 3)
            for par in range(2):
                act.wait_ge(out_done[par], 16 * DT // 2)

        @block.vector
        def _(dve):
            def dyn(ten, k):
                return ten[:, k, :] if isinstance(k, int) else ten[:, bass.ds(k, 1), :].rearrange("p a t -> p (a t)")

            dve.wait_ge(const, 3 + LEVELS)
            dve.wait_ge(cols_ready, 1)
            lg = cols[:, LOGIT:LOGIT + 3 * HH].rearrange("p (l h) -> p l h", l=3)
            dve.tensor_tensor(lbt[:, 3, :], lg[:, 0], lg[:, 1], ALU.max).then_inc(lb_step, 1)
            dve.wait_ge(lb_step, 1)
            dve.tensor_tensor(lbt[:, 4, :], lbt[:, 3, :], lg[:, 2], ALU.max).then_inc(lb_step, 1)
            dve.wait_ge(lb_step, 2)
            dve.tensor_tensor(lbt[:, 0:3, :], lg, lbt[:, 4:5, :].to_broadcast([P, 3, HH]),
                              ALU.subtract).then_inc(lb_step, 1)
            dve.wait_ge(lb_exp, 1)
            dve.tensor_tensor(lbt[:, 3, :], lbt[:, 0, :], lbt[:, 1, :], ALU.add).then_inc(lb_step, 1)
            dve.wait_ge(lb_step, 4)
            dve.tensor_tensor(lbt[:, 4, :], lbt[:, 3, :], lbt[:, 2, :], ALU.add).then_inc(lb_step, 1)
            dve.wait_ge(lb_step, 5)
            dve.reciprocal(lbt[:, 3, :], lbt[:, 4, :]).then_inc(lb_step, 1)
            dve.wait_ge(lb_step, 6)
            dve.tensor_tensor(lbt[:, 4, :], lbt[:, 0, :], lbt[:, 3, :], ALU.mult).then_inc(lb_step, 1)
            dve.wait_ge(lb_step, 7)
            dve.tensor_scalar(lbt[:, 5, :], lbt[:, 4, :], -1.0, 1.0, ALU.mult, ALU.add).then_inc(lb_step, 1)
            dve.tensor_scalar(nbg[:, :], cols[:, BG:BG + GH], -1.0, None, ALU.mult).then_inc(nb_ready, 1)
            for c in range(NC):
                dve.wait_ge(x_turned, c + 1)
                ps = pb if c % 2 else pa
                dve.tensor_copy(xT[:, :, c * P:(c + 1) * P],
                                ps[:, :, :].rearrange("p k (d t) -> p (k d) t", d=4)).then_inc(x_stored, 1)

            def diag_of(m_rs, count, dst, done):
                dve.wait_ge(m_rs, count)
                dve.tensor_tensor(tok(dst), ident[:, :].unsqueeze(1).to_broadcast([P, NC, P]),
                                  rs[:, :].unsqueeze(2).to_broadcast([P, NC, P]), ALU.mult).then_inc(done, 1)

            dve.wait_ge(x_sq, NC)
            dve.tensor_scalar(ms[:, :], ssq[:, :], 1.0 / D, EPS, ALU.mult, ALU.add).then_inc(xn.ms, 1)
            diag_of(xn.rs, 1, aux[:, :], xn.dg)

            def h_lo_of(d, gains, count):
                dve.wait_ge(xn.hi, count)
                dve.scalar_tensor_tensor(dyn(h_lo, d), dyn(xT, d), cols[:, bass.ds(d + gains, 1)],
                                         dyn(h_hi, d).bitcast(F32), ALU.mult, ALU.subtract).then_inc(xn.lo, 1)

            dve.wait_ge(x_stored, NC)
            for d in range(DT):
                h_lo_of(d, MIX, d + 1)
            dve.wait_ge(xn.ready, 1)

            def scaled(t, dst):
                dve.wait_ge(tile_done, t.count(1))
                dve.tensor_tensor(halves(dst), pair(t), rms2(), ALU.mult).then_inc(evac, 1)

            def gate_of(m, h):
                return fg[:, 0:T] if m is mh else dyn(o, h + 4)

            def decay0(m, h):
                dve.wait_ge(m.diag, h + 1)
                dve.tensor_tensor(qp[:, :], qp[:, :], gate_of(m, h), ALU.mult).then_inc(m.decayed, 1)

            def decay(m, h, j):
                b = 1 << j
                dve.wait_ge(m.level, h * 7 + (j + 1))
                dve.wait_ge(m.decayed, h * STEPS + (1 + 2 * j))
                if j:
                    dve.wait_ge(m.blocks, h * 7 + j)
                dve.wait_ge(m.merged, h * 8 + (1 + j))
                g = gate_of(m, h) if j == 0 else fg[:, goff(j):goff(j) + (T >> j)]
                g = g.rearrange("p (k two) -> p k two", two=2)
                for buf, mine, other in ((qp, 1, 0), (ks, 0, 1)):
                    v = buf[:, :].rearrange("p (k s) -> p k s", s=2 * b)[:, :, mine * b:(mine + 1) * b]
                    dve.tensor_tensor(v, v, g[:, :, other:other + 1].to_broadcast([P, T // (2 * b), b]),
                                      ALU.mult).then_inc(m.decayed, 1)

            def merge_diag(m, h, first):
                if not first:
                    dve.wait_ge(m.o_done, h if m is mh else h * 2)
                dve.tensor_tensor(sc[:, :, :], pa[:, :, :].rearrange("p k (c t) -> p (k c) t", c=4),
                                  ident[:, :].unsqueeze(1).to_broadcast([P, NC, P]), ALU.mult).then_inc(m.merged, 1)

            def merge(m, h, j):
                b = 1 << j
                dst = sc[:, :, :].rearrange("p c (k s) -> p c k s", s=2 * b)[:, :, :, b:]
                src = pa[:, j % 2, :].rearrange("p (c k s) -> p c k s", c=NC, s=b)
                msk = mask[:, j, :].rearrange("p (k s) -> p k s", s=b).unsqueeze(1).to_broadcast([P, NC, 64 // b, b])
                dve.copy_predicated(dst, msk, src).then_inc(m.merged, 1)

            def level_done(m, h, j):
                decay(m, h, j)
                merge(m, h, j)

            def states(m, h, st, width):
                dve.wait_ge(m.decayed, h * STEPS + STEPS)
                dve.wait_ge(m.blocks, h * 7 + 7)
                per = HALF // width
                for c in range(7):
                    if m is mh:
                        dve.wait_ge(m.u, h * 2 + 2)
                        bank = c // per
                    else:
                        dve.wait_ge(m.u, h * 4 + (c // 2 + 1))
                        bank = 1 - (c // per) % 2
                    src = pa[:, bank, (c % per) * width:(c % per + 1) * width]
                    if c == 0:
                        dve.tensor_copy(st[:, 0, :], src).then_inc(m.states, 1)
                    else:
                        dve.wait_ge(m.states, h * 7 + c)
                        dve.scalar_tensor_tensor(st[:, c, :], st[:, c - 1, :], g128[:, c:c + 1], src,
                                                 ALU.mult, ALU.add).then_inc(m.states, 1)

            def mean_sq(m, h, count, dv):
                dve.wait_ge(m.stats, count)
                dve.tensor_scalar(ms[:, :], pa[:, 1, 0:NC], 1.0 / dv, EPS, ALU.mult, ALU.add).then_inc(m.ms, 1)

            def o_norm(m, h, tiles):
                dve.wait_ge(m.bc, h + 1)
                for k in tiles:
                    dve.tensor_tensor(halves(dyn(o, k)), halves(dyn(o, k)), pb[:, :, :], ALU.mult).then_inc(m.onorm, 1)

            def hgrn(t, h, first):
                p = h - 1
                if not first:
                    level_done(mh, p, 6)
                    states(mh, p, stH, P)
                    dve.wait_ge(mh.vt, h * 2)
                scaled(t, z[:, 0, :])
                if not first:
                    dve.wait_ge(mh.o_done, h)
                    dve.wait_ge(mh.kt_t, h * 2)
                dve.wait_ge(mh.sig_f, h + 1)
                dve.tensor_scalar(fg[:, 0:T], sg[:, :], lbt[:, 5, bass.ds(h, 1)], lbt[:, 4, bass.ds(h, 1)],
                                  ALU.mult, ALU.add).then_inc(mh.f_ready, 1)
                dve.wait_ge(mh.f_ready, h + 1)
                dve.tensor_scalar(ks[:, :], fg[:, 0:T], -1.0, 1.0, ALU.mult, ALU.add).then_inc(mh.k_ready, 1)
                if not first:
                    dve.wait_ge(mh.gated, h)
                scaled(t.plus(1), z[:, 1, :])
                if not first:
                    mean_sq(mh, p, h, P)
                dve.wait_ge(mh.sig_q, h + 1)
                dve.scalar_tensor_tensor(qp[:, :], z[:, 1, :], SCALE, sg[:, :], ALU.mult,
                                         ALU.mult).then_inc(mh.q_ready, 1)
                if not first:
                    diag_of(mh.rs, h, dg, mh.dg)
                    o_norm(mh, p, (p,))
                dve.wait_ge(mh.q_ready, h + 1)
                decay0(mh, h)
                merge_diag(mh, h, first)
                level_done(mh, h, 0)
                scaled(t.plus(2), z[:, 0, :])
                for j in range(1, 5):
                    level_done(mh, h, j)
                if not first:
                    scaled(t.plus(3), z[:, 1, :])
                level_done(mh, h, 5)

            dve.wait_ge(lb_step, 8)
            hgrn(Tile(N_H), 0, True)
            with dve.Fori(1, HH) as h:
                hgrn(Tile(N_H - 1, 4, h), h, False)
            last = HH - 1
            level_done(mh, last, 6)
            states(mh, last, stH, P)
            dve.wait_ge(mh.gated, HH)
            scaled(Tile(N_HO - 1), z[:, 1, :])

            def split_out(m, order, first):
                for at_k, k in enumerate(order):
                    dve.wait_ge(m.r_hi, first + at_k + 1)
                    dve.tensor_tensor(r_lo[:, k, :], o[:, k, :], r_hi[:, k, :].bitcast(F32),
                                      ALU.subtract).then_inc(m.r_lo, 1)

            split_out(mh, [0, 1, 2], 0)
            mean_sq(mh, last, HH, P)
            split_out(mh, [4, 5], 3)
            diag_of(mh.rs, HH, dg, mh.dg)
            split_out(mh, [6], 5)
            o_norm(mh, last, (last,))
            split_out(mh, [3, 7], 6)

            def x_factor(norm):
                dve.wait_ge(xn.stats, DT * norm)
                dve.tensor_scalar(ms[:, :], pa[:, 1, 0:NC], 1.0 / D, EPS, ALU.mult, ALU.add).then_inc(xn.ms, 1)
                diag_of(xn.rs, norm + 1, aux[:, :], xn.dg)
                dve.wait_ge(xn.ready, norm + 1)

            def to_x(n0, norm=None, final=False):
                def one(t, d):
                    dve.wait_ge(tile_done, t.count(1))
                    xs = dyn(xT, d)
                    if final:
                        par = t.slot() ^ (n0 % 2)
                        if not (isinstance(d, int) and d < 2):
                            dve.wait_ge(out_t, d - 1)
                        dve.tensor_tensor(halves(z[:, par, :]), halves(xs), pair(t), ALU.add).then_inc(evac, 1)
                    else:
                        dve.tensor_tensor(halves(xs), halves(xs), pair(t), ALU.add).then_inc(evac, 1)
                    if norm is not None:
                        gains = MIX + DT if norm == 2 else FFN + DT * (norm // 2)
                        h_lo_of(d, gains, d + (DT * norm + 1))

                one(Tile(n0), 0)
                one(Tile(n0 + 1), 1)
                with dve.Fori(1, DT // 2) as i:
                    one(Tile(n0, 2, i), i * 2)
                    one(Tile(n0 + 1, 2, i), i * 2 + 1)

            to_x(N_HO, norm=1)

            def mlp(l, n0, norm):
                for f0, k, n, nd, end in ffn_starts(n0):
                    def pair_(t, i, first, f0=f0):
                        if not first:
                            dve.wait_ge(ff[l].r_lo, i + f0)
                        scaled(t, z[:, 0, :])
                        dve.wait_ge(ff[l].sig, i + (f0 + 1))
                        dve.tensor_tensor(z[:, 0, :], z[:, 0, :], sg[:, :], ALU.mult).then_inc(ff[l].gate, 1)
                        scaled(t.plus(1), z[:, 1, :])
                        dve.wait_ge(evac, t.count(2))
                        dve.tensor_tensor(z[:, 0, :], z[:, 0, :], z[:, 1, :], ALU.mult).then_inc(ff[l].hid, 1)
                    lead = 1 if f0 == 0 else 0
                    if lead:
                        x_factor(norm)
                        pair_(Tile(n), 0, True)
                    with dve.Fori(lead, k) as i:
                        pair_(Tile(n, 2, i), i, False)
                    to_x(nd, norm=norm + 1 if end and l == 0 else None, final=end and l == 1)

            mlp(0, N_F0, 1)

            x_factor(2)
            dve.wait_ge(tile_done, N_GK + 1)
            dve.tensor_tensor(halves(aux[0:RANK, :]), pair(Tile(N_GK))[0:RANK], halves(rms_x[0:RANK, :]),
                              ALU.mult).then_inc(evac, 1)

            def queries(t, h):
                dve.wait_ge(tile_done, t.count(1))
                dve.scalar_tensor_tensor(halves(qp[:, :]), pair(t), SCALE, rms2(), ALU.mult, ALU.mult).then_inc(evac, 1)

            def keys(t):
                scaled(t, ks[:, :])

            def g_levels(t, h, first):
                dve.wait_ge(f_part, h + 1)
                dve.wait_ge(evac, t.count(4))
                decay0(mg, h)
                merge_diag(mg, h, first)
                level_done(mg, h, 0)
                level_done(mg, h, 1)

            scaled(Tile(N_G), z[:, 0, :])
            scaled(Tile(N_G + 1), z[:, 1, :])
            queries(Tile(N_G + 2), 0)
            keys(Tile(N_G + 3))
            g_levels(Tile(N_G), 0, True)
            for j in range(2, 7):
                level_done(mg, 0, j)

            def gla(t, h):
                p = h - 1
                states(mg, p, stG, 2 * P)
                dve.wait_ge(mg.gated, h * 2 - 1)
                scaled(t, z[:, 0, :])
                scaled(t.plus(1), z[:, 1, :])
                mean_sq(mg, p, h * 2, 2 * P)
                diag_of(mg.rs, h, dg, mg.dg)
                dve.wait_ge(mg.o_done, h * 2)
                queries(t.plus(2), h)
                o_norm(mg, p, (h * 2 - 2, h * 2 - 1))
                keys(t.plus(3))
                g_levels(t, h, False)
                dve.wait_ge(mg.vt, h * 4 + 4)
                scaled(t.plus(4), z[:, 0, :])
                for j in range(2, 6):
                    level_done(mg, h, j)
                scaled(t.plus(5), z[:, 1, :])
                level_done(mg, h, 6)

            with dve.Fori(1, GH) as h:
                gla(Tile(N_G - 2, 6, h), h)
            states(mg, GH - 1, stG, 2 * P)
            dve.wait_ge(mg.gated, 2 * GH - 1)
            scaled(Tile(N_GO - 2), z[:, 0, :])
            scaled(Tile(N_GO - 1), z[:, 1, :])
            split_out(mg, [0, 1, 2], 0)
            mean_sq(mg, GH - 1, 2 * GH, 2 * P)
            split_out(mg, [4, 5], 3)
            diag_of(mg.rs, GH, dg, mg.dg)
            o_norm(mg, GH - 1, (2 * GH - 2, 2 * GH - 1))
            split_out(mg, [3, 6, 7], 5)
            to_x(N_GO, norm=3)
            mlp(1, N_F1, 3)

        @block.gpsimd
        def _(pool):
            def dyn(ten, k):
                return ten[:, k, :] if isinstance(k, int) else ten[:, bass.ds(k, 1), :].rearrange("p a t -> p (a t)")

            pool.memset(ones[:, :], 1.0).then_inc(const, 1)
            pool.wait_ge(const, 1)
            pool.affine_select(ident[:, :], ones[:, :], [[-1, P]], ALU.is_equal, 0.0, base=0,
                               channel_multiplier=1).then_inc(const, 1)
            pool.memset(mhalf[:, :], -0.5).then_inc(const, 1)
            for j in range(LEVELS):
                b = 1 << j
                m0 = qp[:, 64 * j:64 * j + 64].rearrange("p (k s) -> p k s", s=b)
                src = ones[:, 0:64].rearrange("p (k s) -> p k s", s=b)
                pool.affine_select(m0, src, [[-2 * b, 64 // b], [0, b]], ALU.is_ge, 0.0, base=0,
                                   channel_multiplier=1).then_inc(mask_step, 1)
                pool.wait_ge(mask_step, 2 * j + 1)
                pool.affine_select(m0, m0, [[2 * b, 64 // b], [0, b]], ALU.is_ge, 0.0, base=b - 1,
                                   channel_multiplier=-1).then_inc(mask_step, 1)
                pool.wait_ge(mask_step, 2 * j + 2)
                pool.tensor_copy(mask[:, j, :].rearrange("p (k s) -> p k s", s=b), m0).then_inc(const, 1)
            pool.sem_inc(mh.gated, 1)
            pool.sem_inc(mg.gated, 1)

            def split(t):
                pool.wait_ge(hi_ready, t.count(1))
                pool.tensor_tensor(w_lo[:, t.slot(), :, :], w_raw[:, t.slot(), :, :],
                                   w_hi[:, t.slot(), :, :].bitcast(F32), ALU.subtract).then_inc(lo_ready, 1)

            def step(t):
                split(t.plus(2))

            def power(ms_ready, count, done):
                pool.wait_ge(ms_ready, count)
                pool.tensor_tensor(rs[:, :], ms[:, :], mhalf[:, :], ALU.pow).then_inc(done, 1)

            pool.wait_ge(const, 3)
            split(Tile(0))
            split(Tile(1))
            power(xn.ms, 1, xn.rs)

            def block_gates(m, h):
                for j in range(7):
                    if j:
                        pool.wait_ge(m.blocks, h * 7 + j)
                    src = (fg[:, 0:T] if m is mh else dyn(o, h + 4)) if j == 0 else fg[:, goff(j):goff(j) + (T >> j)]
                    src = src.rearrange("p (k two) -> p k two", two=2)
                    pool.tensor_tensor(fg[:, goff(j + 1):goff(j + 1) + (T >> (j + 1))].unsqueeze(2),
                                       src[:, :, 0:1], src[:, :, 1:2], ALU.mult).then_inc(m.blocks, 1)

            def gate(m, slot, sig, n_gs, o_tile, onorm):
                pool.wait_ge(m.sig_g, sig)
                pool.tensor_tensor(sg[:, :], z[:, slot, :], sg[:, :], ALU.mult).then_inc(m.gs, 1)
                pool.wait_ge(m.gs, n_gs)
                pool.wait_ge(m.onorm, onorm)
                pool.tensor_tensor(o_tile, o_tile, sg[:, :], ALU.mult).then_inc(m.gated, 1)

            def hgrn(t, h, first):
                step(t)
                pool.wait_ge(mh.f_ready, h + 1)
                block_gates(mh, h)
                step(t.plus(1))
                if not first:
                    power(mh.ms, h, mh.rs)
                step(t.plus(2))
                if not first:
                    step(t.plus(3))
                    gate(mh, 1, h, h, dyn(o, h - 1), h)

            hgrn(Tile(N_H), 0, True)
            with pool.Fori(1, HH) as h:
                hgrn(Tile(N_H - 1, 4, h), h, False)
            step(Tile(N_HO - 1))
            power(mh.ms, HH, mh.rs)
            gate(mh, 1, HH, HH, o[:, HH - 1, :], HH)

            def to_x(n0, final=False):
                pairs = DT // 2 - (1 if final else 0)
                with pool.Fori(0, pairs) as i:
                    step(Tile(n0, 2, i))
                    step(Tile(n0 + 1, 2, i))

            to_x(N_HO)

            def mlp(l, n0, norm):
                for f0, k, n, nd, end in ffn_starts(n0):
                    def pair_(t, i, f0=f0):
                        step(t)
                        step(t.plus(1))
                        pool.wait_ge(ff[l].r_hi, i + (f0 + 1))
                        pool.tensor_tensor(dyn(r_lo, i), z[:, 0, :], dyn(r_hi, i).bitcast(F32),
                                           ALU.subtract).then_inc(ff[l].r_lo, 1)
                    lead = 1 if f0 == 0 else 0
                    if lead:
                        power(xn.ms, norm + 1, xn.rs)
                        pair_(Tile(n), 0)
                    with pool.Fori(lead, k) as i:
                        pair_(Tile(n, 2, i), i)
                    to_x(nd, final=end and l == 1)

            mlp(0, N_F0, 1)
            power(xn.ms, 3, xn.rs)

            def gla_forget(h):
                pool.wait_ge(mg.sig_f, h + 1)
                pool.tensor_tensor(o[:, 4 + h, :], o[:, 4 + h, :], sg[:, :], ALU.mult).then_inc(f_part, 1)

            step(Tile(N_GK))
            step(Tile(N_G))
            gla_forget(0)
            step(Tile(N_G + 1))
            gla_forget(1)
            gla_forget(2)
            step(Tile(N_G + 2))
            gla_forget(3)
            step(Tile(N_G + 3))
            pool.wait_ge(f_part, GH)
            block_gates(mg, 0)

            def gla(t, h):
                step(t)
                step(t.plus(1))
                power(mg.ms, h, mg.rs)
                step(t.plus(2))
                step(t.plus(3))
                pool.wait_ge(mg.o_done, h * 2)
                block_gates(mg, h)
                step(t.plus(4))
                gate(mg, 0, h * 2 - 1, h * 2 - 1, dyn(o, h * 2 - 2), h * 2 - 1)
                step(t.plus(5))
                gate(mg, 1, h * 2, h * 2, dyn(o, h * 2 - 1), h * 2)

            with pool.Fori(1, GH) as h:
                gla(Tile(N_G - 2, 6, h), h)
            step(Tile(N_GO - 2))
            step(Tile(N_GO - 1))
            power(mg.ms, GH, mg.rs)
            gate(mg, 0, 2 * GH - 1, 2 * GH - 1, o[:, 2 * GH - 2, :], 2 * GH - 1)
            gate(mg, 1, 2 * GH, 2 * GH, o[:, 2 * GH - 1, :], 2 * GH)
            to_x(N_GO)
            mlp(1, N_F1, 3)


_INS = ["x", "norm_mix", "norm_ffn", "hgrn_w_in", "hgrn_g_norm", "hgrn_w_out", "hgrn_lb_logits", "gla_w_in",
        "gla_w_gk_up", "gla_b_gk", "gla_g_norm", "gla_w_out", "ffn_w_gate_up", "ffn_w_down"]


def kernel(**inputs):
    import numpy as _np
    import concourse.bacc as _bacc
    from concourse import mybir as _mybir
    from concourse.bass_utils import run_bass_kernel_spmd as _run

    nc = _bacc.Bacc("TRN2", target_bir_lowering=False, num_devices=1)
    arrays, args = {}, []
    for name in _INS:
        a = _np.ascontiguousarray(inputs[name])
        arrays[f"in_{name}_dram"] = a
        args.append(nc.dram_tensor(f"in_{name}_dram", a.shape, _mybir.dt.from_np(a.dtype), kind="ExternalInput").ap())
    shape = tuple(int(s) for s in inputs["x"].shape)
    args.append(nc.dram_tensor("out_0_dram", shape, _mybir.dt.float32, kind="ExternalOutput").ap())
    trunk(nc, *args)
    r = _run(nc, [arrays], core_ids=[0])
    return r.results[0]["out_0_dram"]
```

```python
from contextlib import ExitStack

import concourse.bass as bass
from concourse import mybir

ALU = mybir.AluOpType
ACT = mybir.ActivationFunctionType
F32 = mybir.dt.float32
F32R = mybir.dt.float32r
U8 = mybir.dt.uint8

P = 128
EPS = 1e-6


class Tile:

    def __init__(self, c, m=0, i=0):
        self.c, self.m, self.i = c, m, i

    def plus(self, k):
        return Tile(self.c + k, self.m, self.i)

    def count(self, k):
        return self.c + k + (self.i * self.m if self.m else 0)

    def slot(self):
        return self.c % 2

    def landed(self):
        return 16 * (self.c // 2 + 1) + (self.i * (8 * self.m) if self.m else 0)


class NormSignals:

    def __init__(self, sem):
        self.sq = sem("xn_sq")
        self.sum = sem("xn_sum")
        self.stats = sem("xn_stats")
        self.parts = sem("xn_parts")
        self.hi = sem("xn_hi")
        self.lo = sem("xn_lo")
        self.ms = sem("xn_ms")
        self.rs = sem("xn_rs")
        self.dg = sem("xn_dg")
        self.bc = sem("xn_bc")
        self.ready = sem("xn_ready")


class MixerSignals:

    def __init__(self, sem, prefix):
        self.f_ready = sem(prefix + "f_ready")
        self.k_ready = sem(prefix + "k_ready")
        self.q_ready = sem(prefix + "q_ready")
        self.sig_f = sem(prefix + "sig_f")
        self.sig_q = sem(prefix + "sig_q")
        self.sig_g = sem(prefix + "sig_g")
        self.blocks = sem(prefix + "blocks")
        self.prod = sem(prefix + "prod")
        self.prod_hi = sem(prefix + "prod_hi")
        self.prod_lo = sem(prefix + "prod_lo")
        self.diag = sem(prefix + "diag")
        self.level = sem(prefix + "level")
        self.decayed = sem(prefix + "decayed")
        self.merged = sem(prefix + "merged")
        self.vt = sem(prefix + "vt")
        self.vn = sem(prefix + "vn")
        self.kt_t = sem(prefix + "kt_t")
        self.kt_c = sem(prefix + "kt_c")
        self.u = sem(prefix + "u")
        self.states = sem(prefix + "states")
        self.intra = sem(prefix + "intra")
        self.o_done = sem(prefix + "o_done")
        self.o_sq = sem(prefix + "o_sq")
        self.o_out = sem(prefix + "o_out")
        self.sq_sum = sem(prefix + "sq_sum")
        self.stats = sem(prefix + "stats")
        self.ms = sem(prefix + "ms")
        self.rs = sem(prefix + "rs")
        self.parts = sem(prefix + "parts")
        self.dg = sem(prefix + "dg")
        self.bc = sem(prefix + "bc")
        self.onorm = sem(prefix + "onorm")
        self.gs = sem(prefix + "gs")
        self.gated = sem(prefix + "gated")
        self.r_hi = sem(prefix + "r_hi")
        self.r_lo = sem(prefix + "r_lo")


class MlpSignals:

    def __init__(self, sem, prefix):
        self.sig = sem(prefix + "sig")
        self.gate = sem(prefix + "gate")
        self.hid = sem(prefix + "hid")
        self.r_hi = sem(prefix + "r_hi")
        self.r_lo = sem(prefix + "r_lo")


def trunk(nc, x, norm_mix, norm_ffn, hgrn_w_in, hgrn_g_norm, hgrn_w_out, hgrn_lb_logits,
          gla_w_in, gla_w_gk_up, gla_b_gk, gla_g_norm, gla_w_out, ffn_w_gate_up, ffn_w_down, out):
    T, D = x.shape[1], x.shape[2]
    DT = D // P
    NC = T // P
    HALF = T // 2
    HH = D // P
    GH = 4
    GK = GH * P
    RANK = gla_w_gk_up.shape[1]
    FH = ffn_w_down.shape[1]
    FT = FH // P
    GROUPS = [8, 8, FT - 16]
    LEVELS = 7
    ALIGNED = 64
    STEPS = 1 + 2 * LEVELS
    SCALE = float(P) ** -0.5
    assert T == 1024 and DT == 8 and FT == 22 and NC == 8

    ctx = ExitStack()
    with ctx:
        base = (nc.sbuf_base + 63) // 64 * 64
        at = [base]

        def place(name, shape, dt=F32, offset=None):
            nbytes = 1
            for s in shape[1:]:
                nbytes *= s
            nbytes *= 1 if dt == U8 else 4
            if offset is None:
                offset = at[0]
                at[0] += (nbytes + 31) // 32 * 32
            return nc.alloc_sbuf_tensor_at(name, shape, dt, offset=offset)

        xT = place("xT", [P, DT, T])
        h_hi = place("h_hi", [P, DT, T], F32R)
        h_lo = place("h_lo", [P, DT, T], F32R)
        w_raw = place("w_raw", [P, 2, 8, P])
        w_hi = place("w_hi", [P, 2, 8, P], F32R)
        w_lo = place("w_lo", [P, 2, 8, P], F32R)
        rms_x = place("rms_x", [P, T])
        z_at = at[0]
        z = place("z", [P, 2, T])
        z_r = place("z_r", [P, 2, T], F32R, z_at)
        sg = place("sg", [P, T])
        aux_at = at[0]
        aux = place("aux", [P, T])
        dg_lo = place("dg_lo", [P, T], F32R, aux_at)
        o_at = at[0]
        o = place("o", [P, DT, T])
        s_at = at[0]
        qp = place("qp", [P, T])
        ks = place("ks", [P, T])
        sc_at = at[0]
        sc = place("sc", [P, NC, P])
        own_hi = place("own_hi", [P, T], F32R, sc_at)
        kt_at = at[0]
        kt = place("kt", [P, T])
        dg_hi = place("dg_hi", [P, T], F32R, kt_at)
        fg = place("fg", [P, 2 * T])
        vn = place("vn", [P, 2 * T])
        r_lo = place("r_lo", [P, DT, T], F32R, o_at)
        r_hi = place("r_hi", [P, DT, T], F32R, s_at)
        ident = place("ident", [P, P])
        ones = place("ones", [P, P])
        cols = place("cols", [P, 64])
        mask = place("mask", [P, LEVELS, P // 2], U8)
        mhalf = place("mhalf", [P, NC])
        ms = place("ms", [P, NC])
        rs = place("rs", [P, NC])
        rs_hi = place("rs_hi", [P, NC], F32R)
        rs_lo = place("rs_lo", [P, NC])
        ones_r = place("ones_r", [P, P], F32R)
        ssq = place("ssq", [P, NC])
        lbt = place("lbt", [P, 6, HH])
        nbg = place("nbg", [P, GH])
        rows = z[0:63, 0, 0:P]
        used = at[0] - base
        assert at[0] <= nc.sbuf_usable_end, (at[0], nc.sbuf_usable_end)
        ctx.enter_context(nc.sbuf_tensor("arena", [P, used + 64], U8))
        MIX, FFN, LOGIT, HG, GG, BG = 0, 16, 32, 56, 57, 59

        pp = ctx.enter_context(nc.psum_tensor("pp", [P, 4, HALF], F32))
        pa = ctx.enter_context(nc.psum_tensor("pa", [P, 2, HALF], F32))
        pb = ctx.enter_context(nc.psum_tensor("pb", [P, 2, HALF], F32))

        def sem(name):
            return ctx.enter_context(nc.semaphore(name))

        landed = [sem("landed0"), sem("landed1")]
        hi_ready, lo_ready = sem("hi_ready"), sem("lo_ready")
        tile_done, evac, asked = sem("tile_done"), sem("evac"), sem("asked")
        rows_in, x_in, up_in = sem("rows_in"), [sem(f"x_in{c}") for c in range(NC)], sem("up_in")
        const, mask_step, cols_t, cols_ready = sem("const"), sem("mask_step"), sem("cols_t"), sem("cols_ready")
        lb_step, lb_exp, nb_ready = sem("lb_step"), sem("lb_exp"), sem("nb_ready")
        x_turned, x_stored, x_sq = sem("x_turned"), sem("x_stored"), sem("x_sq")
        x_hi, x_lo = sem("x_hi"), sem("x_lo")
        xn = NormSignals(sem)
        out_t, out_c, out_done = sem("out_t"), sem("out_c"), [sem("out_done0"), sem("out_done1")]
        mh, mg = MixerSignals(sem, "h_"), MixerSignals(sem, "g_")
        zf, zs, f_part = sem("zf"), sem("zs"), sem("f_part")
        ff = [MlpSignals(sem, f"ff{l}_") for l in range(2)]

        def halves(ap):
            return ap.rearrange("p (k t) -> p k t", k=2)

        def tok(ap):
            return ap.rearrange("p (c t) -> p c t", c=NC)

        def pair(t):
            return pp[:, 2 * t.slot():2 * t.slot() + 2, :]

        def rms2():
            return halves(rms_x[:, :])

        def goff(j):
            return 2 * T - ((2 * T) >> j)

        sq = kt[:, :]
        g128 = fg[:, goff(7):goff(7) + NC]
        stH = fg[:, 0:7 * P].rearrange("p (c v) -> p c v", c=7)
        stG = fg[:, 0:7 * 2 * P].rearrange("p (c v) -> p c v", c=7)
        vnH = vn[:, 0:NC * P].rearrange("p (c v) -> p c v", c=NC)
        vnG = vn[:, :].rearrange("p (c v) -> p c v", c=NC)
        ktc = tok(kt[:, :])

        def wcols(w, k0, n, col, width=P):
            return w[k0 * P:(k0 + n) * P, bass.ds(col, width)].rearrange("(k p) c -> p k c", p=P)

        W_H, W_G = hgrn_w_in[0], gla_w_in[0]
        N_H = 0
        N_HO = N_H + 4 * HH
        N_F0 = N_HO + DT
        FFN_TILES = 2 * FT + 3 * DT
        N_GK = N_F0 + FFN_TILES
        N_G = N_GK + 1
        N_GO = N_G + 6 * GH
        N_F1 = N_GO + DT
        N_END = N_F1 + FFN_TILES

        def ffn_starts(n0):
            res, n, f0 = [], n0, 0
            for g, k in enumerate(GROUPS):
                res.append((f0, k, n, n + 2 * k, g == len(GROUPS) - 1))
                n += 2 * k + DT
                f0 += k
            return res

        ORDER_H = [1, 5, 2, 6, 0, 4, 3, 7]
        ORDER_G = [1, 0, 2, 4, 5, 3, 6, 7]

        block = ctx.enter_context(nc.Block())

        @block.sync
        def _(sp):
            def load_rows(*parts):
                for at_row, src in parts:
                    sp.dma_start(z[at_row:at_row + src.shape[0], 0, 0:P], src).then_inc(rows_in, 16)

            xv = x.rearrange("b (c p) d -> (b c) p d", p=P)

            def load_x(c):
                sp.dma_start(o[:, c, :], xv[c]).then_inc(x_in[c], 16)

            load_x(0)
            load_rows((MIX, norm_mix.rearrange("l (t p) -> (l t) p", p=P)),
                      (FFN, norm_ffn.rearrange("l (t p) -> (l t) p", p=P)),
                      (LOGIT, hgrn_lb_logits.rearrange("l (t p) -> (l t) p", p=P)))
            load_x(1)
            load_rows((HG, hgrn_g_norm), (GG, gla_g_norm.rearrange("l (t p) -> (l t) p", p=P)),
                      (BG, gla_b_gk.rearrange("l (t p) -> (l t) p", p=P)))

            def load(t, w, col, k0=0, n=8, width=P):
                if not (t.m == 0 and t.c < 2):
                    sp.wait_ge(lo_ready, t.count(-1))
                    sp.sem_inc(asked, 1)
                sp.dma_start(w_raw[:, t.slot(), 0:n, 0:width],
                             wcols(w, k0, n, col, width)).then_inc(landed[t.slot()], 16)

            def hgrn_loads(t, h):
                load(t, W_H, h * P + D)
                load(t.plus(1), W_H, h * P)
                load(t.plus(2), W_H, h * P + 2 * D)

            def mlp_loads(n0, l):
                for f0, k, n, nd, _ in ffn_starts(n0):
                    with sp.Fori(0, k) as i:
                        load(Tile(n, 2, i), ffn_w_gate_up[l], i * P + f0 * P)
                        load(Tile(n + 1, 2, i), ffn_w_gate_up[l], i * P + (f0 * P + FH))
                    with sp.Fori(0, DT // 2) as i:
                        load(Tile(nd, 2, i), ffn_w_down[l], i * (2 * P), f0, k)
                        load(Tile(nd + 1, 2, i), ffn_w_down[l], i * (2 * P) + P, f0, k)

            for c in range(2, NC // 2):
                load_x(c)
            load(Tile(N_H), W_H, D)
            for c in range(NC // 2, NC):
                load_x(c)
            load(Tile(N_H + 1), W_H, 0)
            load(Tile(N_H + 2), W_H, 2 * D)
            with sp.Fori(1, HH) as h:
                hgrn_loads(Tile(N_H - 1, 4, h), h)
                load(Tile(N_H + 2, 4, h), W_H, h * P + (3 * D - P))
            load(Tile(N_HO - 1), W_H, 4 * D - P)
            with sp.Fori(0, DT // 2) as i:
                load(Tile(N_HO, 2, i), hgrn_w_out[0], i * (2 * P))
                load(Tile(N_HO + 1, 2, i), hgrn_w_out[0], i * (2 * P) + P)
            mlp_loads(N_F0, 0)

            load(Tile(N_GK), W_G, 2 * GK + 2 * D, width=RANK)
            load(Tile(N_G), W_G, 0)
            sp.wait_ge(tile_done, N_GK)
            sp.dma_start(o[0:RANK, 0, 0:GK], gla_w_gk_up[0]).then_inc(up_in, 16)

            def gla_loads(t, h):
                load(t, W_G, h * (2 * P) + 2 * GK)
                load(t.plus(1), W_G, h * (2 * P) + (2 * GK + P))
                load(t.plus(2), W_G, h * P)
                load(t.plus(3), W_G, h * P + GK)

            for k, col in enumerate((GK, 2 * GK, 2 * GK + P)):
                load(Tile(N_G + 1 + k), W_G, col)
            with sp.Fori(1, GH) as h:
                gla_loads(Tile(N_G - 2, 6, h), h)
                load(Tile(N_G + 2, 6, h), W_G, h * (2 * P) + (2 * GK + D - 2 * P))
                load(Tile(N_G + 3, 6, h), W_G, h * (2 * P) + (2 * GK + D - P))
            load(Tile(N_GO - 2), W_G, 2 * GK + 2 * D - 2 * P)
            load(Tile(N_GO - 1), W_G, 2 * GK + 2 * D - P)
            with sp.Fori(0, DT // 2) as i:
                load(Tile(N_GO, 2, i), gla_w_out[0], i * (2 * P))
                load(Tile(N_GO + 1, 2, i), gla_w_out[0], i * (2 * P) + P)
            mlp_loads(N_F1, 1)

        @block.tensor
        def _(pe):
            def weights_ready(t):
                pe.wait_ge(lo_ready, t.count(1))
                if not (t.m == 0 and t.c < 2):
                    pe.wait_ge(evac, t.count(-1))

            def passes(t, hi, lo, k, first, last):
                s = t.slot()
                for w, act, st, sp_ in ((w_hi, hi, first, False), (w_hi, lo, False, False),
                                        (w_lo, hi, False, last)):
                    for half in range(2):
                        mm = pe.matmul(pp[:, 2 * s + half, :], w[:, s, k, :],
                                       act[:, k, half * HALF:(half + 1) * HALF], start=st, stop=sp_)
                if last:
                    mm.then_inc(tile_done, 1)

            def tile(t, hi, lo, n=8, slots=None, ready=None):
                slots = slots or {}
                weights_ready(t)
                for k in range(n):
                    if ready:
                        ready(k)
                    passes(t, hi, lo, k, k == 0, k == n - 1)
                    for emit in slots.get(k, ()):
                        emit()

            def first_outputs(n0, order, early, m, slots):
                for part in (order[:early], order[early:]):
                    for j in range(2):
                        if part[0] == order[0]:
                            weights_ready(Tile(n0 + j))
                        for k in part:
                            pe.wait_ge(m.r_lo, order.index(k) + 1)
                            passes(Tile(n0 + j), r_hi, r_lo, k, k == order[0], k == order[-1])
                            for emit in slots.get((j, k), ()):
                                emit()

            def diagonal(m, h):
                pe.wait_ge(m.prod_lo, h * 2 + 1)
                if not isinstance(h, int) or h > 0:
                    pe.wait_ge(m.states, h * 7)
                    pe.wait_ge(m.ms, h)
                for half in range(2):
                    for part, lo in ((own_hi[:, :], False), (z_r[:, 0, :], True)):
                        mm = pe.matmul(pa[:, half, :], ones_r[:, :], part[:, half * HALF:(half + 1) * HALF],
                                       start=not lo, stop=lo)
                mm.then_inc(m.diag, 1)

            def level0(m, h):
                pe.wait_ge(m.prod_lo, h * 2 + 2)
                pe.wait_ge(m.merged, h * 8 + 1)
                pe.matmul(pa[:, 0, :], ones_r[:, :], z_r[:, 1, HALF:T], start=True, stop=False)
                pe.matmul(pa[:, 0, :], ones_r[:, :], z_r[:, 1, 0:HALF], start=False, stop=True).then_inc(m.level, 1)

            def level(m, h, j):
                if j == 0:
                    level0(m, h)
                    return
                b = 1 << j
                pe.wait_ge(m.decayed, h * STEPS + (1 + 2 * j))
                pe.wait_ge(m.merged, h * 8 + j)
                qv = qp[:, :].rearrange("p (c k s) -> p c k s", c=NC, s=2 * b)[:, :, :, b:]
                for c in range(NC):
                    if b < ALIGNED:
                        mm = pe.matmul(pa[:, j % 2, c * 64:(c + 1) * 64].rearrange("p (k s) -> p k s", s=b),
                                       ks[:, c * P:(c + 1) * P], qv[:, c], start=True, stop=True)
                        continue
                    for k in range(64 // b):
                        mm = pe.matmul(pa[2 * b * k:2 * b * k + b, j % 2, c * 64 + b * k:c * 64 + b * k + b],
                                       ks[:, c * P + 2 * b * k:c * P + 2 * b * k + b], qv[:, c, k],
                                       start=True, stop=True)
                mm.then_inc(m.level, 1)

            def turn_keys(m, h):
                pe.wait_ge(m.decayed, h * STEPS + STEPS)
                for bank in (1, 0):
                    pe.wait_ge(m.merged, h * 8 + (7 if bank else 8))
                    if bank == 1 and m is mh:
                        pe.wait_ge(m.vn, h * 2 + 1)
                    if bank == 0 and m is mh:
                        pe.wait_ge(m.vn, h * 2 + 2)
                    for c in range(4 * bank, 4 * bank + 4):
                        mm = pe.transpose(pa[:, bank, (c % 4) * P:(c % 4 + 1) * P],
                                          ks[:, c * P:(c + 1) * P], ident[:, :])
                    mm.then_inc(m.kt_t, 1)

            def updates(h):
                pe.wait_ge(mh.kt_c, h * 2 + 2)
                for bank in (1, 0):
                    cs = range(4, 7) if bank else range(0, 4)
                    for c in cs:
                        mm = pe.matmul(pa[:, bank, (c % 4) * P:(c % 4 + 1) * P], ktc[:, c, :], vnH[:, c, :],
                                       start=True, stop=True)
                    mm.then_inc(mh.u, 1)

            def updates_g(h, part):
                pe.wait_ge(mg.kt_c, h * 2 + 2)
                for q in range(2):
                    if part:
                        pe.wait_ge(mg.states, h * 7 + 2 * (q + 1))
                    for c in (4 * part + 2 * q, 4 * part + 2 * q + 1):
                        if c < 7:
                            mm = pe.matmul(pa[:, 1 - q, (c % 2) * 256:(c % 2 + 1) * 256], ktc[:, c, :],
                                           vnG[:, c, :], start=True, stop=True)
                    mm.then_inc(mg.u, 1)

            def intra(m, h, val):
                pe.wait_ge(m.merged, h * 8 + 8)
                for c in range(NC):
                    mm = pe.matmul(pb[:, c // 4, (c % 4) * P:(c % 4 + 1) * P], val(c), sc[:, c, :],
                              start=(c % 4 == 0), stop=(c == 0), skip_group_check=True)
                mm.then_inc(m.intra, 1)

            def inter(m, h, st):
                pe.wait_ge(m.states, h * 7 + 7)
                for c in range(1, NC):
                    mm = pe.matmul(pb[:, c // 4, (c % 4) * P:(c % 4 + 1) * P], st(c - 1), qp[:, c * P:(c + 1) * P],
                                   start=False, stop=True, skip_group_check=True)
                mm.then_inc(m.o_done, 1)

            def stats_of(ps, src, done):
                for c in range(NC):
                    mm = pe.matmul(ps[:, c:c + 1], src[:, c * P:(c + 1) * P], ones[:, 0:1],
                                   start=True, stop=True)
                mm.then_inc(done, 1)

            def spread(done):
                for half in range(2):
                    for src in (dg_hi, dg_lo):
                        mm = pe.matmul(pb[:, half, :], ones_r[:, :], src[:, half * HALF:(half + 1) * HALF],
                                       start=(src is dg_hi), stop=(src is dg_lo))
                mm.then_inc(done, 1)

            pe.wait_ge(const, 2)
            pe.wait_ge(rows_in, 96)
            pe.transpose(pp[:, 0, 0:63], rows, ident[0:63, 0:63]).then_inc(cols_t, 1)
            def turn_x(c):
                pe.wait_ge(x_in[c], 16)
                ps = pb if c % 2 else pa
                if c >= 2:
                    pe.wait_ge(x_stored, c - 1)
                for d in range(DT):
                    mm = pe.transpose(ps[:, d // 4, (d % 4) * P:(d % 4 + 1) * P], o[:, c, d * P:(d + 1) * P],
                                      ident[:, :])
                mm.then_inc(x_turned, 1)

            def first_tile():
                for c in range(6):
                    turn_x(c)
                pe.wait_ge(cols_ready, 1)
                pe.wait_ge(lo_ready, 1)
                for half in range(2):
                    for k in range(DT):
                        pe.wait_ge(xn.lo if half else x_lo, k + 1)
                        for w, act in ((w_hi, h_hi), (w_hi, h_lo), (w_lo, h_hi)):
                            mm = pe.matmul(pp[:, half, :], w[:, 0, k, :], act[:, k, half * HALF:(half + 1) * HALF],
                                           start=(k == 0 and w is w_hi and act is h_hi),
                                           stop=(k == DT - 1 and w is w_lo))
                        if half == 0 and k in (1, 3):
                            turn_x(6 if k == 1 else 7)
                mm.then_inc(tile_done, 1)

            def h_ready(norm):
                def ready(k):
                    pe.wait_ge(xn.lo, DT * norm + k + 1)
                return ready

            def x_stats(norm):
                def emit():
                    pe.wait_ge(xn.sum, 7 * norm)
                    stats_of(pa[:, 1, :], aux[:, :], xn.stats)
                return emit

            def x_spread(norm):
                def emit():
                    pe.wait_ge(xn.dg, 2 * norm + 2)
                    spread(xn.bc)
                return emit

            def turn_values(h):
                for bank in (1, 0):
                    pe.wait_ge(mh.merged, h * 8 + (7 if bank else 8))
                    if bank == 1:
                        pe.wait_ge(evac, zi_count(h))
                    for c in range(4 * bank, 4 * bank + 4):
                        mm = pe.transpose(pa[:, bank, (c % 4) * P:(c % 4 + 1) * P], z[:, 0, c * P:(c + 1) * P],
                                          ident[:, :])
                    mm.then_inc(mh.vt, 1)

            def zi_count(h):
                return 3 if isinstance(h, int) and h == 0 else h * 4 + 2

            def h_intra(h, later):
                if later:
                    pe.wait_ge(mh.onorm, h)
                else:
                    pe.wait_ge(xn.ready, 1)
                intra(mh, h, lambda c: vnH[:, c, :])

            def h_stats(h):
                pe.wait_ge(mh.o_sq, h + 1)
                stats_of(pa[:, 1, :], sq, mh.stats)

            def h_spread(h):
                pe.wait_ge(mh.dg, h * 2 + 2)
                pe.wait_ge(mh.o_out, h + 1)
                spread(mh.bc)

            def hgrn(t, h, later):
                p = h - 1
                tail = {0: [lambda: level(mh, p, 5)], 2: [lambda: level(mh, p, 6)], 4: [lambda: turn_values(p)],
                        6: [lambda: turn_keys(mh, p)]}
                if not later:
                    tail = {0: [lambda: level(mh, p, 1)], 1: [lambda: level(mh, p, 2)], 2: [lambda: level(mh, p, 3)],
                            3: [lambda: level(mh, p, 4)], 4: [lambda: level(mh, p, 5)], 5: [lambda: level(mh, p, 6)],
                            6: [lambda: turn_values(p)], 7: [lambda: turn_keys(mh, p)]}
                tile(t, h_hi, h_lo, slots=tail)
                tile(t.plus(1), h_hi, h_lo, slots={
                    0: [lambda: updates(p)], 2: [lambda: h_intra(p, later)],
                    4: [lambda: inter(mh, p, lambda c: stH[:, c, :])],
                    7: [lambda: h_stats(p)]})
                tile(t.plus(2), h_hi, h_lo, slots={
                    5: [lambda: diagonal(mh, h)], 7: [lambda: level(mh, h, 0)]})
                tile(t.plus(3), h_hi, h_lo, slots={
                    0: [lambda: level(mh, h, 1)], 2: [lambda: level(mh, h, 2)], 3: [lambda: h_spread(p)],
                    4: [lambda: level(mh, h, 3)], 6: [lambda: level(mh, h, 4)]})

            first_tile()
            tile(Tile(N_H + 1), h_hi, h_lo, slots={4: [x_spread(0)]})
            tile(Tile(N_H + 2), h_hi, h_lo, slots={
                5: [lambda: diagonal(mh, 0)], 7: [lambda: level(mh, 0, 0)]})
            hgrn(Tile(N_H + 3), 1, False)
            with pe.Fori(2, HH) as h:
                hgrn(Tile(N_H - 1, 4, h), h, True)
            last = HH - 1
            tile(Tile(N_HO - 1), h_hi, h_lo, slots={
                0: [lambda: level(mh, last, 5)], 1: [lambda: level(mh, last, 6)], 2: [lambda: turn_values(last)],
                3: [lambda: turn_keys(mh, last)], 4: [lambda: updates(last)], 6: [lambda: h_intra(last, True)]})
            inter(mh, last, lambda c: stH[:, c, :])

            def to_x(n0, n, ready=None, final=False, first=0):
                def slot(d_done, par):
                    return {3: [turn_out(d_done, par)]} if final else {}

                if not first:
                    tile(Tile(n0), r_hi, r_lo, n, ready=ready)
                    tile(Tile(n0 + 1), r_hi, r_lo, n, slots=slot(1, 0))
                with pe.Fori(1, DT // 2) as i:
                    tile(Tile(n0, 2, i), r_hi, r_lo, n, slots=slot(i * 2, 1))
                    tile(Tile(n0 + 1, 2, i), r_hi, r_lo, n, slots=slot(i * 2 + 1, 0))

            def turn_out(d_done, par):
                def emit():
                    first = isinstance(d_done, int) and d_done == 1
                    pe.wait_ge(evac, d_done + (N_END - DT))
                    if not first:
                        pe.wait_ge(out_c, d_done - 1)
                    for c in range(NC):
                        mm = pe.transpose(pa[:, c // 4, (c % 4) * P:(c % 4 + 1) * P],
                                          z[:, par, c * P:(c + 1) * P], ident[:, :])
                    mm.then_inc(out_t, 1)
                return emit

            first_outputs(N_HO, ORDER_H, 5, mh, {(0, ORDER_H[1]): [lambda: h_stats(last)],
                                                 (1, ORDER_H[0]): [lambda: h_spread(last)]})
            to_x(N_HO, 8, first=2)

            def mlp(l, n0, norm):
                for f0, k, n, nd, end in ffn_starts(n0):
                    lead = 1 if f0 == 0 else 0
                    if lead:
                        tile(Tile(n), h_hi, h_lo, ready=h_ready(norm),
                             slots={4: [x_stats(norm)]})
                        tile(Tile(n + 1), h_hi, h_lo, slots={0: [x_spread(norm)]})
                    with pe.Fori(lead, k) as i:
                        tile(Tile(n, 2, i), h_hi, h_lo)
                        tile(Tile(n + 1, 2, i), h_hi, h_lo)

                    def hid_ready(kk, f0=f0):
                        pe.wait_ge(ff[l].r_lo, f0 + kk + 1)
                    to_x(nd, k, hid_ready, final=end and l == 1)

            mlp(0, N_F0, 1)

            def z_gate(h):
                def emit():
                    ps = pb if h else pa
                    if h == 0:
                        pe.wait_ge(up_in, 16)
                        pe.wait_ge(evac, N_GK + 1)
                        pe.wait_ge(xn.ms, 3)
                    if h == 1:
                        pe.wait_ge(xn.ready, 3)
                    if h >= 2:
                        pe.wait_ge(zs, 5 * h)
                    for half in range(2):
                        mm = pe.matmul(ps[:, half, :], o[0:RANK, 0, h * P:(h + 1) * P],
                                       o[0:RANK, 1, half * HALF:(half + 1) * HALF], start=True, stop=True)
                    mm.then_inc(zf, 1)
                return emit

            def g_turn_values(h, j):
                for bank in (0, 1):
                    if j == 0:
                        pe.wait_ge(evac, N_G + 3 if isinstance(h, int) and h == 0 else h * 6 + (N_G - 1))
                        if isinstance(h, int) and h == 0:
                            pe.wait_ge(mg.merged, 8 - bank)
                        else:
                            pe.wait_ge(mg.states, h * 7)
                            pe.wait_ge(mg.ms, h)
                    else:
                        pe.wait_ge(evac, N_G + 4 if isinstance(h, int) and h == 0 else h * 6 + N_G)
                        pe.wait_ge(mg.vn, h * 4 + bank + 1)
                    for c in range(4 * bank, 4 * bank + 4):
                        mm = pe.transpose(pa[:, bank, (c % 4) * P:(c % 4 + 1) * P], z[:, j, c * P:(c + 1) * P],
                                          ident[:, :])
                    mm.then_inc(mg.vt, 1)

            def g_diag(h):
                if isinstance(h, int) and h == 0:
                    pe.wait_ge(zs, 5)
                else:
                    pe.wait_ge(mg.vn, h * 4 + 4)
                diagonal(mg, h)

            def g_intra(h, j, later=True):
                if j == 0 and later:
                    pe.wait_ge(mg.onorm, h * 2)
                elif j == 0:
                    pe.wait_ge(zs, 5 * GH)
                if j == 1:
                    pe.wait_ge(mg.o_out, h * 2 + 1)
                intra(mg, h, lambda c: vnG[:, c, j * P:(j + 1) * P])

            def g_inter(h, j):
                inter(mg, h, lambda c: stG[:, c, j * P:(j + 1) * P])

            def g_stats(h):
                pe.wait_ge(mg.sq_sum, h + 1)
                stats_of(pa[:, 1, :], sq, mg.stats)

            def g_spread(h):
                pe.wait_ge(mg.dg, h * 2 + 2)
                pe.wait_ge(mg.o_out, h * 2 + 2)
                spread(mg.bc)

            def g_levels(h):
                return ({4: [lambda: g_diag(h)], 6: [lambda: level(mg, h, 0)], 7: [lambda: level(mg, h, 1)]},
                        {1: [lambda: level(mg, h, 2)], 3: [lambda: level(mg, h, 3)],
                         5: [lambda: level(mg, h, 4)], 7: [lambda: level(mg, h, 5)]})

            def gla(t, h, later):
                p = h - 1
                if later:
                    tail = {0: [lambda: level(mg, p, 6)], 2: [lambda: turn_keys(mg, p)], 4: [lambda: updates_g(p, 0)],
                            6: [lambda: updates_g(p, 1)], 7: [lambda: g_intra(p, 0, True)]}
                else:
                    tail = {0: [lambda: level(mg, p, 6)], 1: [lambda: g_turn_values(p, 0)],
                            2: [lambda: g_turn_values(p, 1)],
                            4: [lambda: pe.wait_ge(mg.vn, 4), lambda: turn_keys(mg, p)],
                            5: [lambda: updates_g(p, 0)], 6: [lambda: updates_g(p, 1)],
                            7: [lambda: g_intra(p, 0, False)]}
                tile(t, h_hi, h_lo, slots=tail)
                tile(t.plus(1), h_hi, h_lo, slots={1: [lambda: g_inter(p, 0)],
                                                   5: [lambda: g_intra(p, 1), lambda: g_inter(p, 1)]})
                tile(t.plus(2), h_hi, h_lo, slots={2: [lambda: g_stats(p)], 7: [lambda: g_turn_values(h, 0)]})
                tile(t.plus(3), h_hi, h_lo, slots={1: [lambda: g_spread(p)], 3: [lambda: g_turn_values(h, 1)]})
                a, b = g_levels(h)
                tile(t.plus(4), h_hi, h_lo, slots=a)
                tile(t.plus(5), h_hi, h_lo, slots=b)

            tile(Tile(N_GK), h_hi, h_lo, ready=h_ready(2), slots={4: [x_stats(2)]})
            tile(Tile(N_G), h_hi, h_lo, slots={0: [x_spread(2)], 3: [z_gate(0)], 6: [z_gate(1)]})
            tile(Tile(N_G + 1), h_hi, h_lo)
            a, b = g_levels(0)
            a[5] = [z_gate(2)]
            b[3] = [z_gate(3)] + b[3]
            tile(Tile(N_G + 2), h_hi, h_lo, slots=a)
            tile(Tile(N_G + 3), h_hi, h_lo, slots=b)
            gla(Tile(N_G + 4), 1, False)
            with pe.Fori(2, GH) as h:
                gla(Tile(N_G - 2, 6, h), h, True)
            lastg = GH - 1
            tile(Tile(N_GO - 2), h_hi, h_lo, slots={
                0: [lambda: level(mg, lastg, 6)], 1: [lambda: turn_keys(mg, lastg)], 3: [lambda: updates_g(lastg, 0)],
                4: [lambda: updates_g(lastg, 1)], 6: [lambda: g_intra(lastg, 0)], 7: [lambda: g_inter(lastg, 0)]})
            tile(Tile(N_GO - 1), h_hi, h_lo, slots={
                2: [lambda: g_intra(lastg, 1), lambda: g_inter(lastg, 1)], 5: [lambda: g_stats(lastg)]})
            first_outputs(N_GO, ORDER_G, 5, mg, {(0, ORDER_G[3]): [lambda: g_spread(lastg)]})
            to_x(N_GO, 8, first=2)
            mlp(1, N_F1, 3)
            turn_out(DT, 1)()

        @block.scalar
        def _(act):
            def split(t):
                act.wait_ge(landed[t.slot()], t.landed())
                if not (t.m == 0 and t.c < 2):
                    act.wait_ge(tile_done, t.count(-1))
                act.activation(w_hi[:, t.slot(), :, :], w_raw[:, t.slot(), :, :], ACT.Copy).then_inc(hi_ready, 1)

            def step(t):
                split(t.plus(2))

            def first_split(k):
                act.wait_ge(landed[k], 16)
                act.activation(w_hi[:, k, :, :], w_raw[:, k, :, :], ACT.Copy).then_inc(hi_ready, 1)

            act.wait_ge(cols_t, 1)
            act.activation(cols[:, 0:63], pp[:, 0, 0:63], ACT.Copy).then_inc(cols_ready, 1)
            act.wait_ge(lb_step, 3)
            act.activation(lbt[:, 0:3, :], lbt[:, 0:3, :], ACT.Exp).then_inc(lb_exp, 1)

            def x_squares(c):
                act.wait_ge(x_in[c], 16)
                if c:
                    act.wait_ge(x_sq, c)
                act.activation(sg[:, :], o[:, c, :], ACT.Square, accum_out=ssq[:, c:c + 1]).then_inc(x_sq, 1)

            def first_hi(half):
                act.wait_ge(x_stored, 4 * half + 4)
                for d in range(DT):
                    t0 = half * HALF
                    act.activation(h_hi[:, d, t0:t0 + HALF], xT[:, d, t0:t0 + HALF], ACT.Copy,
                                   scale=cols[:, MIX + d:MIX + d + 1]).then_inc(xn.hi if half else x_hi, 1)

            for c in range(3):
                x_squares(c)
            first_split(0)
            act.wait_ge(cols_ready, 1)
            first_hi(0)
            x_squares(3)
            x_squares(4)
            first_split(1)
            first_hi(1)
            for c in range(5, NC):
                x_squares(c)

            def store_rms(norm):
                act.wait_ge(xn.bc, norm + 1)
                if norm:
                    act.wait_ge(evac, {1: N_F0, 2: N_GK, 3: N_F1}[norm])
                act.activation(rms2(), pb[:, :, :], ACT.Copy).then_inc(xn.ready, 1)

            act.wait_ge(landed[0], 32)
            act.wait_ge(tile_done, 1)
            act.activation(w_hi[:, 0, :, :], w_raw[:, 0, :, :], ACT.Copy).then_inc(hi_ready, 1)
            store_rms(0)

            def keys_copy(m, h, first):
                if not first:
                    act.wait_ge(m.bc, h)
                for q, bank in enumerate((1, 0)):
                    act.wait_ge(m.kt_t, h * 2 + q + 1)
                    act.activation(kt[:, bank * HALF:(bank + 1) * HALF], pa[:, bank, :], ACT.Copy).then_inc(m.kt_c, 1)

            def values_copy(h, first):
                if not first:
                    act.wait_ge(mh.o_done, h)
                for q, bank in enumerate((1, 0)):
                    act.wait_ge(mh.vt, h * 2 + q + 1)
                    act.activation(vnH[:, 4 * bank:4 * bank + 4, :],
                                   pa[:, bank, :].rearrange("p (c v) -> p c v", c=4), ACT.Copy).then_inc(mh.vn, 1)

            def out_copy(m, n_done, o_tile, col, sq_to):
                act.wait_ge(m.o_done, n_done)
                act.activation(halves(sq_to), pb[:, :, :], ACT.Square).then_inc(m.o_sq, 1)
                act.activation(halves(o_tile), pb[:, :, :], ACT.Copy, scale=col).then_inc(m.o_out, 1)

            def products_hi(m, h):
                act.wait_ge(m.prod, h * 2 + 1)
                act.activation(own_hi[:, :], z[:, 0, :], ACT.Copy).then_inc(m.prod_hi, 1)
                act.wait_ge(m.prod, h * 2 + 2)
                act.activation(z_r[:, 1, HALF:T], z[:, 1, 0:HALF], ACT.Copy).then_inc(m.prod_hi, 1)

            def o_tile(k):
                return o[:, bass.ds(k, 1), :].rearrange("p a t -> p (a t)") if not isinstance(k, int) else o[:, k, :]

            def sigmoid(t, slot, done, dst=sg):
                act.wait_ge(evac, t.count(1))
                act.activation(dst[:, :], z[:, slot, :], ACT.Sigmoid).then_inc(done, 1)

            def hgrn(t, h, first):
                p = h - 1
                if not first:
                    values_copy(p, isinstance(h, int) and h == 1)
                    keys_copy(mh, p, isinstance(h, int) and h == 1)
                    step(t)
                    act.wait_ge(mh.q_ready, h)
                    act.wait_ge(mh.gated, h)
                sigmoid(t, 0, mh.sig_f)
                if not first:
                    out_copy(mh, h, o_tile(p), cols[:, HG:HG + 1], sq)
                step(t.plus(1))
                act.wait_ge(mh.f_ready, h + 1)
                sigmoid(t.plus(1), 1, mh.sig_q)
                products_hi(mh, h)
                step(t.plus(2))
                if not first:
                    step(t.plus(3))
                    act.wait_ge(mh.q_ready, h + 1)
                    sigmoid(t.plus(3), 1, mh.sig_g)

            hgrn(Tile(N_H), 0, True)
            hgrn(Tile(N_H + 3), 1, False)
            with act.Fori(2, HH) as h:
                hgrn(Tile(N_H - 1, 4, h), h, False)
            last = HH - 1
            values_copy(last, False)
            keys_copy(mh, last, False)
            def split_out(m, order, waits):
                for k in order:
                    for w in waits.get(k, ()):
                        act.wait_ge(*w)
                    act.activation(r_hi[:, k, :], o[:, k, :], ACT.Copy).then_inc(m.r_hi, 1)

            act.wait_ge(mh.gated, HH)
            split_out(mh, ORDER_H[:4], {5: [(mh.states, 7 * HH)], 2: [(mh.intra, HH)]})
            act.wait_ge(mh.o_done, HH)
            act.activation(halves(sq), pb[:, :, :], ACT.Square).then_inc(mh.o_sq, 1)
            step(Tile(N_HO - 1))
            act.activation(halves(o[:, last, :]), pb[:, :, :], ACT.Copy, scale=cols[:, HG:HG + 1]).then_inc(mh.o_out, 1)
            split_out(mh, ORDER_H[4:6], {})
            sigmoid(Tile(N_HO - 1), 1, mh.sig_g)
            split_out(mh, ORDER_H[6:], {3: [(mh.bc, HH)], 7: [(mh.gated, HH + 1)]})

            def to_x(n0, norm=None, final=False):
                def one(t, d):
                    step_t = not (final and t.m == 0 and t.c + 2 >= N_END)
                    if step_t:
                        step(t)
                    if norm is not None:
                        gains = MIX + DT if norm == 2 else FFN + DT * (norm // 2)
                        xs = xT[:, d, :] if isinstance(d, int) else xT[:, bass.ds(d, 1), :].rearrange("p a t -> p (a t)")
                        hi = h_hi[:, d, :] if isinstance(d, int) else h_hi[:, bass.ds(d, 1), :].rearrange("p a t -> p (a t)")
                        if not (isinstance(d, int) and d < 2):
                            act.wait_ge(xn.sum, d + (7 * (norm - 1) - 1))
                        act.wait_ge(evac, t.count(1))
                        act.activation(hi, xs, ACT.Copy, scale=cols[:, bass.ds(d + gains, 1)]).then_inc(xn.hi, 1)
                        sq_to = aux if isinstance(d, int) and d == 0 else sg
                        act.activation(sq_to[:, :], xs, ACT.Square).then_inc(xn.sq, 1)
                    if final:
                        par = t.slot() ^ (n0 % 2)
                        act.wait_ge(out_t, d + 1)
                        if not (isinstance(d, int) and d < 2):
                            act.wait_ge(out_done[par], (d - par) * 8)
                        stage = (sg if par == 0 else aux)[:, :]
                        act.activation(halves(stage), pa[:, :, :], ACT.Copy).then_inc(out_c, 1)
                        act.wait_ge(out_c, d + 1)
                        dst = out[0].rearrange("(c p) d -> p c d", p=P)[:, :, bass.ds(d * P, P)]
                        act.dma_start(dst, tok(stage)).then_inc(out_done[par], 16)

                if final:
                    one(Tile(n0), 0)
                    one(Tile(n0 + 1), 1)
                    with act.Fori(1, DT // 2 - 1) as i:
                        one(Tile(n0, 2, i), i * 2)
                        one(Tile(n0 + 1, 2, i), i * 2 + 1)
                    one(Tile(n0 + DT - 2), DT - 2)
                    one(Tile(n0 + DT - 1), DT - 1)
                else:
                    one(Tile(n0), 0)
                    one(Tile(n0 + 1), 1)
                    with act.Fori(1, DT // 2) as i:
                        one(Tile(n0, 2, i), i * 2)
                        one(Tile(n0 + 1, 2, i), i * 2 + 1)

            to_x(N_HO, norm=1)

            def mlp(l, n0, norm):
                for f0, k, n, nd, end in ffn_starts(n0):
                    def pair_(t, i, f0=f0):
                        step(t)
                        act.wait_ge(evac, t.count(1))
                        act.activation(sg[:, :], z[:, 0, :], ACT.Sigmoid).then_inc(ff[l].sig, 1)
                        step(t.plus(1))
                        act.wait_ge(ff[l].hid, i + (f0 + 1))
                        dst = r_hi[:, i, :] if isinstance(i, int) else r_hi[:, bass.ds(i, 1), :].rearrange(
                            "p a t -> p (a t)")
                        act.activation(dst, z[:, 0, :], ACT.Copy).then_inc(ff[l].r_hi, 1)
                    lead = 1 if f0 == 0 else 0
                    if lead:
                        store_rms(norm)
                        pair_(Tile(n), 0)
                    with act.Fori(lead, k) as i:
                        pair_(Tile(n, 2, i), i)
                    to_x(nd, norm=norm + 1 if end and l == 0 else None, final=end and l == 1)

            mlp(0, N_F0, 1)

            def gate_parts(h):
                ps = (pb if h else pa)[:, :, :]
                act.wait_ge(zf, h + 1)
                if h:
                    act.wait_ge(f_part, h)
                f = o[:, 4 + h, :]
                act.activation(halves(sg[:, :]), ps, ACT.Abs, bias=cols[:, BG + h:BG + h + 1]).then_inc(zs, 1)
                act.wait_ge(zs, 5 * h + 1)
                act.activation(sg[:, :], sg[:, :], ACT.Exp, scale=-1.0).then_inc(zs, 1)
                act.wait_ge(zs, 5 * h + 2)
                act.activation(sg[:, :], sg[:, :], ACT.Ln, bias=1.0).then_inc(zs, 1)
                act.wait_ge(zs, 5 * h + 3)
                act.activation(f, sg[:, :], ACT.Exp, scale=-1.0 / 16).then_inc(zs, 1)
                act.wait_ge(zs, 5 * h + 4)
                act.activation(halves(sg[:, :]), ps, ACT.Relu, scale=-1.0, bias=nbg[:, h:h + 1]).then_inc(zs, 1)
                act.wait_ge(zs, 5 * h + 5)
                act.activation(sg[:, :], sg[:, :], ACT.Exp, scale=-1.0 / 16).then_inc(mg.sig_f, 1)

            store_rms(2)
            act.wait_ge(nb_ready, 1)
            step(Tile(N_GK))
            gate_parts(0)
            step(Tile(N_G))
            gate_parts(1)
            step(Tile(N_G + 1))
            products_hi(mg, 0)
            step(Tile(N_G + 2))
            gate_parts(2)
            gate_parts(3)
            step(Tile(N_G + 3))
            act.wait_ge(f_part, GH)

            def g_values_copy(h, j):
                for bank in (0, 1):
                    act.wait_ge(mg.vt, h * 4 + 2 * j + bank + 1)
                    act.activation(vnG[:, 4 * bank:4 * bank + 4, j * P:(j + 1) * P],
                                   pa[:, bank, :].rearrange("p (c v) -> p c v", c=4), ACT.Copy).then_inc(mg.vn, 1)

            def g_out(h, j):
                out_copy(mg, h * 2 + j + 1, o_tile(h * 2 + j), cols[:, GG + j:GG + j + 1],
                         aux[:, :] if j else sq)

            def g_gate(t, p, j):
                if j:
                    act.wait_ge(mg.gated, p * 2 + 2)
                sigmoid(t, j, mg.sig_g)

            def gla(t, h):
                p = h - 1
                if isinstance(h, int):
                    g_values_copy(p, 0)
                    g_values_copy(p, 1)
                keys_copy(mg, p, isinstance(h, int) and h == 1)
                step(t)
                g_out(p, 0)
                step(t.plus(1))
                g_out(p, 1)
                step(t.plus(2))
                g_values_copy(h, 0)
                g_values_copy(h, 1)
                step(t.plus(3))
                products_hi(mg, h)
                step(t.plus(4))
                if not (isinstance(h, int) and h == 1):
                    act.wait_ge(mg.gated, p * 2 + 1)
                g_gate(t.plus(4), p, 0)
                step(t.plus(5))
                g_gate(t.plus(5), p, 1)

            gla(Tile(N_G + 4), 1)
            with act.Fori(2, GH) as h:
                gla(Tile(N_G - 2, 6, h), h)
            keys_copy(mg, GH - 1, False)
            step(Tile(N_GO - 2))
            act.wait_ge(mg.gated, 2 * GH - 1)
            sigmoid(Tile(N_GO - 2), 0, mg.sig_g)
            g_out(GH - 1, 0)
            g_out(GH - 1, 1)
            act.wait_ge(mg.gated, 2 * GH - 1)
            split_out(mg, ORDER_G[:5], {})
            step(Tile(N_GO - 1))
            sigmoid(Tile(N_GO - 1), 1, mg.sig_g, rms_x)
            split_out(mg, ORDER_G[5:], {3: [(mg.bc, GH)], 6: [(mg.gated, 2 * GH)], 7: [(mg.gated, 2 * GH + 1)]})
            to_x(N_GO, norm=3)
            mlp(1, N_F1, 3)
            for par in range(2):
                act.wait_ge(out_done[par], 16 * DT // 2)

        @block.vector
        def _(dve):
            def dyn(ten, k):
                return ten[:, k, :] if isinstance(k, int) else ten[:, bass.ds(k, 1), :].rearrange("p a t -> p (a t)")

            dve.wait_ge(cols_ready, 1)
            lg = cols[:, LOGIT:LOGIT + 3 * HH].rearrange("p (l h) -> p l h", l=3)
            dve.tensor_tensor(lbt[:, 3, :], lg[:, 0], lg[:, 1], ALU.max).then_inc(lb_step, 1)
            dve.wait_ge(lb_step, 1)
            dve.tensor_tensor(lbt[:, 4, :], lbt[:, 3, :], lg[:, 2], ALU.max).then_inc(lb_step, 1)
            dve.wait_ge(lb_step, 2)
            dve.tensor_tensor(lbt[:, 0:3, :], lg, lbt[:, 4:5, :].to_broadcast([P, 3, HH]),
                              ALU.subtract).then_inc(lb_step, 1)
            dve.wait_ge(lb_exp, 1)
            dve.tensor_tensor(lbt[:, 3, :], lbt[:, 0, :], lbt[:, 1, :], ALU.add).then_inc(lb_step, 1)
            dve.wait_ge(lb_step, 4)
            dve.tensor_tensor(lbt[:, 4, :], lbt[:, 3, :], lbt[:, 2, :], ALU.add).then_inc(lb_step, 1)
            dve.wait_ge(lb_step, 5)
            dve.reciprocal(lbt[:, 3, :], lbt[:, 4, :]).then_inc(lb_step, 1)
            dve.wait_ge(lb_step, 6)
            dve.tensor_tensor(lbt[:, 4, :], lbt[:, 0, :], lbt[:, 3, :], ALU.mult).then_inc(lb_step, 1)
            dve.wait_ge(lb_step, 7)
            dve.tensor_scalar(lbt[:, 5, :], lbt[:, 4, :], -1.0, 1.0, ALU.mult, ALU.add).then_inc(lb_step, 1)
            dve.tensor_scalar(nbg[:, :], cols[:, BG:BG + GH], -1.0, None, ALU.mult).then_inc(nb_ready, 1)

            def store_x(c):
                dve.wait_ge(x_turned, c + 1)
                ps = pb if c % 2 else pa
                dve.tensor_copy(xT[:, :, c * P:(c + 1) * P],
                                ps[:, :, :].rearrange("p k (d t) -> p (k d) t", d=4)).then_inc(x_stored, 1)

            def first_lo(half, d):
                t0 = half * HALF
                dve.wait_ge(xn.hi if half else x_hi, d + 1)
                dve.scalar_tensor_tensor(h_lo[:, d, t0:t0 + HALF], xT[:, d, t0:t0 + HALF],
                                         cols[:, MIX + d:MIX + d + 1], h_hi[:, d, t0:t0 + HALF].bitcast(F32),
                                         ALU.mult, ALU.subtract).then_inc(xn.lo if half else x_lo, 1)

            for c in range(NC // 2):
                store_x(c)
            dve.wait_ge(x_stored, NC // 2)
            for c in range(NC // 2, NC):
                store_x(c)
                first_lo(0, 2 * c - NC)
                first_lo(0, 2 * c - NC + 1)

            def diag_of(m, n):
                dve.wait_ge(m.rs, n + 1)
                dve.tensor_copy(rs_hi[:, :], rs[:, :]).then_inc(m.parts, 1)
                dve.wait_ge(m.parts, n * 2 + 1)
                dve.tensor_tensor(rs_lo[:, :], rs[:, :], rs_hi[:, :].bitcast(F32), ALU.subtract).then_inc(m.parts, 1)
                for part, dst in ((rs_hi[:, :].bitcast(F32), dg_hi), (rs_lo[:, :], dg_lo)):
                    if dst is dg_lo:
                        dve.wait_ge(m.parts, n * 2 + 2)
                    dve.tensor_tensor(tok(dst[:, :]), ident[:, :].unsqueeze(1).to_broadcast([P, NC, P]),
                                      part.unsqueeze(2).to_broadcast([P, NC, P]), ALU.mult).then_inc(m.dg, 1)

            def h_lo_of(d, gains, count):
                dve.wait_ge(xn.hi, count)
                dve.scalar_tensor_tensor(dyn(h_lo, d), dyn(xT, d), cols[:, bass.ds(d + gains, 1)],
                                         dyn(h_hi, d).bitcast(F32), ALU.mult, ALU.subtract).then_inc(xn.lo, 1)

            dve.wait_ge(x_stored, NC)
            for d in range(DT):
                first_lo(1, d)
            dve.wait_ge(x_sq, NC)
            dve.tensor_scalar(ms[:, :], ssq[:, :], 1.0 / D, EPS, ALU.mult, ALU.add).then_inc(xn.ms, 1)
            diag_of(xn, 0)
            dve.wait_ge(xn.ready, 1)

            def scaled(t, dst):
                dve.wait_ge(tile_done, t.count(1))
                dve.tensor_tensor(halves(dst), pair(t), rms2(), ALU.mult).then_inc(evac, 1)

            def gate_of(m, h):
                return fg[:, 0:T] if m is mh else dyn(o, h + 4)

            def products(m, h):
                dve.tensor_tensor(z[:, 0, :], qp[:, :], ks[:, :], ALU.mult).then_inc(m.prod, 1)
                dve.tensor_tensor(qp[:, :], qp[:, :], gate_of(m, h), ALU.mult).then_inc(m.decayed, 1)
                dve.wait_ge(m.decayed, h * STEPS + 1)
                pairs = [b[:, :].rearrange("p (k two) -> p k two", two=2) for b in (qp, ks)]
                dve.tensor_tensor(z[:, 1, 0:HALF].unsqueeze(2), pairs[0][:, :, 1:2], pairs[1][:, :, 0:1],
                                  ALU.mult).then_inc(m.prod, 1)
                dve.wait_ge(m.prod_hi, h * 2 + 1)
                dve.tensor_tensor(z_r[:, 0, :], z[:, 0, :], own_hi[:, :].bitcast(F32), ALU.subtract).then_inc(m.prod_lo, 1)
                dve.wait_ge(m.prod_hi, h * 2 + 2)
                dve.tensor_tensor(z_r[:, 1, 0:HALF], z[:, 1, 0:HALF], z_r[:, 1, HALF:T].bitcast(F32),
                                  ALU.subtract).then_inc(m.prod_lo, 1)

            def decay(m, h, j, parts=((qp, 1, 0), (ks, 0, 1))):
                b = 1 << j
                if j:
                    dve.wait_ge(m.level, h * 7 + (j + 1))
                if parts[0][0] is qp:
                    dve.wait_ge(m.decayed, h * STEPS + (1 + 2 * j))
                if j:
                    dve.wait_ge(m.blocks, h * 7 + j)
                    dve.wait_ge(m.merged, h * 8 + (1 + j))
                g = gate_of(m, h) if j == 0 else fg[:, goff(j):goff(j) + (T >> j)]
                g = g.rearrange("p (k two) -> p k two", two=2)
                for buf, mine, other in parts:
                    v = buf[:, :].rearrange("p (k s) -> p k s", s=2 * b)[:, :, mine * b:(mine + 1) * b]
                    dve.tensor_tensor(v, v, g[:, :, other:other + 1].to_broadcast([P, T // (2 * b), b]),
                                      ALU.mult).then_inc(m.decayed, 1)

            def merge_diag(m, h):
                dve.wait_ge(m.diag, h + 1)
                dve.tensor_tensor(sc[:, :, :], pa[:, :, :].rearrange("p k (c t) -> p (k c) t", c=4),
                                  ident[:, :].unsqueeze(1).to_broadcast([P, NC, P]), ALU.mult).then_inc(m.merged, 1)

            def merge(m, j):
                b = 1 << j
                if b >= ALIGNED:
                    for k in range(64 // b):
                        lo_p = 2 * b * k
                        last = dve.tensor_copy(sc[lo_p:lo_p + b, :, lo_p + b:lo_p + 2 * b],
                                               pa[lo_p:lo_p + b, j % 2, :].rearrange(
                                                   "p (c s) -> p c s", c=NC)[:, :, b * k:b * k + b])
                    last.then_inc(m.merged, 1)
                    return
                dst = sc[:, :, :].rearrange("p c (k s) -> p c k s", s=2 * b)[:, :, :, b:]
                src = pa[:, j % 2, :].rearrange("p (c k s) -> p c k s", c=NC, s=b)
                msk = mask[:, j, :].rearrange("p (k s) -> p k s", s=b).unsqueeze(1).to_broadcast([P, NC, 64 // b, b])
                dve.copy_predicated(dst, msk, src).then_inc(m.merged, 1)

            def level0_done(m, h):
                decay(m, h, 0, ((qp, 1, 0),))
                merge_diag(m, h)
                dve.wait_ge(m.level, h * 7 + 1)
                dve.wait_ge(m.merged, h * 8 + 1)
                decay(m, h, 0, ((ks, 0, 1),))
                merge(m, 0)

            def level_done(m, h, j):
                decay(m, h, j)
                merge(m, j)

            def states(m, h, st, width):
                dve.wait_ge(m.decayed, h * STEPS + STEPS)
                dve.wait_ge(m.blocks, h * 7 + 7)
                per = HALF // width
                for c in range(7):
                    if m is mh:
                        dve.wait_ge(m.u, h * 2 + 2)
                        bank = c // per
                    else:
                        dve.wait_ge(m.u, h * 4 + (c // 2 + 1))
                        bank = 1 - (c // per) % 2
                    src = pa[:, bank, (c % per) * width:(c % per + 1) * width]
                    if c == 0:
                        dve.tensor_copy(st[:, 0, :], src).then_inc(m.states, 1)
                    else:
                        dve.wait_ge(m.states, h * 7 + c)
                        dve.scalar_tensor_tensor(st[:, c, :], st[:, c - 1, :], g128[:, c:c + 1], src,
                                                 ALU.mult, ALU.add).then_inc(m.states, 1)

            def mean_sq(m, count, dv):
                dve.wait_ge(m.stats, count)
                dve.tensor_scalar(ms[:, :], pa[:, 1, 0:NC], 1.0 / dv, EPS, ALU.mult, ALU.add).then_inc(m.ms, 1)

            def o_norm(m, h, tiles):
                dve.wait_ge(m.bc, h + 1)
                for k in tiles:
                    dve.tensor_tensor(halves(dyn(o, k)), halves(dyn(o, k)), pb[:, :, :], ALU.mult).then_inc(m.onorm, 1)

            def hgrn(t, h, first):
                p = h - 1
                if not first:
                    level_done(mh, p, 6)
                    states(mh, p, stH, P)
                    dve.wait_ge(mh.vt, h * 2)
                scaled(t, z[:, 0, :])
                if not first:
                    dve.wait_ge(mh.o_done, h)
                    dve.wait_ge(mh.kt_t, h * 2)
                dve.wait_ge(mh.sig_f, h + 1)
                dve.tensor_scalar(fg[:, 0:T], sg[:, :], lbt[:, 5, bass.ds(h, 1)], lbt[:, 4, bass.ds(h, 1)],
                                  ALU.mult, ALU.add).then_inc(mh.f_ready, 1)
                dve.wait_ge(mh.f_ready, h + 1)
                dve.tensor_scalar(ks[:, :], fg[:, 0:T], -1.0, 1.0, ALU.mult, ALU.add).then_inc(mh.k_ready, 1)
                if not first:
                    dve.wait_ge(mh.gated, h)
                scaled(t.plus(1), z[:, 1, :])
                if not first:
                    mean_sq(mh, h, P)
                dve.wait_ge(mh.sig_q, h + 1)
                dve.scalar_tensor_tensor(qp[:, :], z[:, 1, :], SCALE, sg[:, :], ALU.mult,
                                         ALU.mult).then_inc(mh.q_ready, 1)
                dve.wait_ge(mh.q_ready, h + 1)
                products(mh, h)
                level0_done(mh, h)
                scaled(t.plus(2), z[:, 0, :])
                level_done(mh, h, 1)
                if not first:
                    diag_of(mh, p)
                level_done(mh, h, 2)
                if not first:
                    o_norm(mh, p, (p,))
                level_done(mh, h, 3)
                level_done(mh, h, 4)
                if not first:
                    scaled(t.plus(3), z[:, 1, :])
                level_done(mh, h, 5)

            dve.wait_ge(lb_step, 8)
            dve.wait_ge(const, 4 + LEVELS)
            hgrn(Tile(N_H), 0, True)
            with dve.Fori(1, HH) as h:
                hgrn(Tile(N_H - 1, 4, h), h, False)
            last = HH - 1
            level_done(mh, last, 6)
            states(mh, last, stH, P)

            def split_out(m, order, first):
                for at_k, k in enumerate(order):
                    dve.wait_ge(m.r_hi, first + at_k + 1)
                    dve.tensor_tensor(r_lo[:, k, :], o[:, k, :], r_hi[:, k, :].bitcast(F32),
                                      ALU.subtract).then_inc(m.r_lo, 1)

            split_out(mh, ORDER_H[:4], 0)
            dve.wait_ge(mh.gated, HH)
            scaled(Tile(N_HO - 1), z[:, 1, :])
            mean_sq(mh, HH, P)
            split_out(mh, ORDER_H[4:6], 4)
            diag_of(mh, HH - 1)
            o_norm(mh, last, (last,))
            split_out(mh, ORDER_H[6:], 6)

            def x_factor(norm):
                dve.wait_ge(xn.stats, norm)
                dve.tensor_scalar(ms[:, :], pa[:, 1, 0:NC], 1.0 / D, EPS, ALU.mult, ALU.add).then_inc(xn.ms, 1)
                diag_of(xn, norm)
                dve.wait_ge(xn.ready, norm + 1)

            def to_x(n0, norm=None, final=False):
                def one(t, d):
                    dve.wait_ge(tile_done, t.count(1))
                    xs = dyn(xT, d)
                    if final:
                        par = t.slot() ^ (n0 % 2)
                        if not (isinstance(d, int) and d < 2):
                            dve.wait_ge(out_t, d - 1)
                        dve.tensor_tensor(halves(z[:, par, :]), halves(xs), pair(t), ALU.add).then_inc(evac, 1)
                    else:
                        dve.tensor_tensor(halves(xs), halves(xs), pair(t), ALU.add).then_inc(evac, 1)
                    if norm is not None:
                        gains = MIX + DT if norm == 2 else FFN + DT * (norm // 2)
                        h_lo_of(d, gains, d + (DT * norm + 1))
                        if not (isinstance(d, int) and d == 0):
                            dve.wait_ge(xn.sq, d + (DT * (norm - 1) + 1))
                            dve.tensor_tensor(aux[:, :], aux[:, :], sg[:, :], ALU.add).then_inc(xn.sum, 1)

                one(Tile(n0), 0)
                one(Tile(n0 + 1), 1)
                with dve.Fori(1, DT // 2) as i:
                    one(Tile(n0, 2, i), i * 2)
                    one(Tile(n0 + 1, 2, i), i * 2 + 1)

            to_x(N_HO, norm=1)

            def mlp(l, n0, norm):
                for f0, k, n, nd, end in ffn_starts(n0):
                    def pair_(t, i, first, f0=f0):
                        if not first:
                            dve.wait_ge(ff[l].r_lo, i + f0)
                        scaled(t, z[:, 0, :])
                        dve.wait_ge(ff[l].sig, i + (f0 + 1))
                        dve.tensor_tensor(z[:, 0, :], z[:, 0, :], sg[:, :], ALU.mult).then_inc(ff[l].gate, 1)
                        scaled(t.plus(1), z[:, 1, :])
                        dve.wait_ge(evac, t.count(2))
                        dve.tensor_tensor(z[:, 0, :], z[:, 0, :], z[:, 1, :], ALU.mult).then_inc(ff[l].hid, 1)
                    lead = 1 if f0 == 0 else 0
                    if lead:
                        x_factor(norm)
                        pair_(Tile(n), 0, True)
                    with dve.Fori(lead, k) as i:
                        pair_(Tile(n, 2, i), i, False)
                    to_x(nd, norm=norm + 1 if end and l == 0 else None, final=end and l == 1)

            mlp(0, N_F0, 1)

            x_factor(2)
            dve.wait_ge(tile_done, N_GK + 1)
            dve.tensor_tensor(halves(o[0:RANK, 1, :]), pair(Tile(N_GK))[0:RANK], halves(rms_x[0:RANK, :]),
                              ALU.mult).then_inc(evac, 1)

            def queries(t):
                dve.wait_ge(tile_done, t.count(1))
                dve.scalar_tensor_tensor(halves(qp[:, :]), pair(t), SCALE, rms2(), ALU.mult, ALU.mult).then_inc(evac, 1)

            def keys(t):
                scaled(t, ks[:, :])

            def g_levels(a, b, count, h, first):
                dve.wait_ge(f_part, h + 1)
                dve.wait_ge(evac, count)
                if not first:
                    dve.wait_ge(mg.vt, h * 4 + 4)
                products(mg, h)
                level0_done(mg, h)
                level_done(mg, h, 1)
                scaled(a, z[:, 0, :])
                for j in range(2, 6):
                    level_done(mg, h, j)
                scaled(b, z[:, 1, :])
                level_done(mg, h, 6)

            queries(Tile(N_G))
            keys(Tile(N_G + 1))
            g_levels(Tile(N_G + 2), Tile(N_G + 3), N_G + 2, 0, True)

            def squares(h):
                dve.wait_ge(mg.o_sq, h * 2 + 2)
                dve.tensor_tensor(sq, sq, aux[:, :], ALU.add).then_inc(mg.sq_sum, 1)

            def gla(t, h):
                p = h - 1
                states(mg, p, stG, 2 * P)
                dve.wait_ge(mg.gated, h * 2 - 1)
                dve.wait_ge(mg.vt, h * 4)
                scaled(t, z[:, 0, :])
                scaled(t.plus(1), z[:, 1, :])
                squares(p)
                mean_sq(mg, h, 2 * P)
                diag_of(mg, p)
                dve.wait_ge(mg.o_done, h * 2)
                queries(t.plus(2))
                o_norm(mg, p, (h * 2 - 2, h * 2 - 1))
                keys(t.plus(3))
                g_levels(t.plus(4), t.plus(5), t.count(4), h, False)

            with dve.Fori(1, GH) as h:
                gla(Tile(N_G - 2, 6, h), h)
            states(mg, GH - 1, stG, 2 * P)
            dve.wait_ge(mg.gated, 2 * GH - 1)
            scaled(Tile(N_GO - 2), z[:, 0, :])
            squares(GH - 1)
            split_out(mg, ORDER_G[:2], 0)
            mean_sq(mg, GH, 2 * P)
            diag_of(mg, GH - 1)
            split_out(mg, ORDER_G[2:4], 2)
            scaled(Tile(N_GO - 1), z[:, 1, :])
            split_out(mg, ORDER_G[4:5], 4)
            o_norm(mg, GH - 1, (2 * GH - 2, 2 * GH - 1))
            split_out(mg, ORDER_G[5:], 5)
            to_x(N_GO, norm=3)
            mlp(1, N_F1, 3)

        @block.gpsimd
        def _(pool):
            def dyn(ten, k):
                return ten[:, k, :] if isinstance(k, int) else ten[:, bass.ds(k, 1), :].rearrange("p a t -> p (a t)")

            pool.memset(ones[:, :], 1.0).then_inc(const, 1)
            pool.wait_ge(const, 1)
            pool.affine_select(ident[:, :], ones[:, :], [[-1, P]], ALU.is_equal, 0.0, base=0,
                               channel_multiplier=1).then_inc(const, 1)
            pool.memset(mhalf[:, :], -0.5).then_inc(const, 1)
            pool.tensor_copy(ones_r[:, :], ones[:, :]).then_inc(const, 1)
            for j in range(LEVELS):
                b = 1 << j
                m0 = qp[:, 64 * j:64 * j + 64].rearrange("p (k s) -> p k s", s=b)
                src = ones[:, 0:64].rearrange("p (k s) -> p k s", s=b)
                pool.affine_select(m0, src, [[-2 * b, 64 // b], [0, b]], ALU.is_ge, 0.0, base=0,
                                   channel_multiplier=1).then_inc(mask_step, 1)
                pool.wait_ge(mask_step, 2 * j + 1)
                pool.affine_select(m0, m0, [[2 * b, 64 // b], [0, b]], ALU.is_ge, 0.0, base=b - 1,
                                   channel_multiplier=-1).then_inc(mask_step, 1)
                pool.wait_ge(mask_step, 2 * j + 2)
                pool.tensor_copy(mask[:, j, :].rearrange("p (k s) -> p k s", s=b), m0).then_inc(const, 1)
            pool.sem_inc(mh.gated, 1)
            pool.sem_inc(mg.gated, 1)

            def split(t):
                pool.wait_ge(hi_ready, t.count(1))
                pool.tensor_tensor(w_lo[:, t.slot(), :, :], w_raw[:, t.slot(), :, :],
                                   w_hi[:, t.slot(), :, :].bitcast(F32), ALU.subtract).then_inc(lo_ready, 1)

            def step(t):
                split(t.plus(2))

            def power(ms_ready, count, done):
                pool.wait_ge(ms_ready, count)
                pool.tensor_tensor(rs[:, :], ms[:, :], mhalf[:, :], ALU.pow).then_inc(done, 1)

            pool.wait_ge(const, 3)
            split(Tile(0))
            split(Tile(1))
            power(xn.ms, 1, xn.rs)

            def block_gates(m, h):
                for j in range(7):
                    if j:
                        pool.wait_ge(m.blocks, h * 7 + j)
                    src = (fg[:, 0:T] if m is mh else dyn(o, h + 4)) if j == 0 else fg[:, goff(j):goff(j) + (T >> j)]
                    src = src.rearrange("p (k two) -> p k two", two=2)
                    pool.tensor_tensor(fg[:, goff(j + 1):goff(j + 1) + (T >> (j + 1))].unsqueeze(2),
                                       src[:, :, 0:1], src[:, :, 1:2], ALU.mult).then_inc(m.blocks, 1)

            def gate(m, slot, sig, n_gs, o_tile, onorm):
                pool.wait_ge(m.sig_g, sig)
                pool.tensor_tensor(sg[:, :], z[:, slot, :], sg[:, :], ALU.mult).then_inc(m.gs, 1)
                pool.wait_ge(m.gs, n_gs)
                pool.wait_ge(m.onorm, onorm)
                pool.tensor_tensor(o_tile, o_tile, sg[:, :], ALU.mult).then_inc(m.gated, 1)

            def hgrn(t, h, first):
                step(t)
                pool.wait_ge(mh.f_ready, h + 1)
                block_gates(mh, h)
                step(t.plus(1))
                if not first:
                    power(mh.ms, h, mh.rs)
                step(t.plus(2))
                if not first:
                    step(t.plus(3))
                    gate(mh, 1, h, h, dyn(o, h - 1), h)

            hgrn(Tile(N_H), 0, True)
            with pool.Fori(1, HH) as h:
                hgrn(Tile(N_H - 1, 4, h), h, False)
            step(Tile(N_HO - 1))
            power(mh.ms, HH, mh.rs)
            gate(mh, 1, HH, HH, o[:, HH - 1, :], HH)

            def to_x(n0, final=False):
                pairs = DT // 2 - (1 if final else 0)
                with pool.Fori(0, pairs) as i:
                    step(Tile(n0, 2, i))
                    step(Tile(n0 + 1, 2, i))

            to_x(N_HO)

            def mlp(l, n0, norm):
                for f0, k, n, nd, end in ffn_starts(n0):
                    def pair_(t, i, f0=f0):
                        step(t)
                        step(t.plus(1))
                        pool.wait_ge(ff[l].r_hi, i + (f0 + 1))
                        pool.tensor_tensor(dyn(r_lo, i), z[:, 0, :], dyn(r_hi, i).bitcast(F32),
                                           ALU.subtract).then_inc(ff[l].r_lo, 1)
                    lead = 1 if f0 == 0 else 0
                    if lead:
                        power(xn.ms, norm + 1, xn.rs)
                        pair_(Tile(n), 0)
                    with pool.Fori(lead, k) as i:
                        pair_(Tile(n, 2, i), i)
                    to_x(nd, final=end and l == 1)

            mlp(0, N_F0, 1)
            power(xn.ms, 3, xn.rs)

            def gla_forget(h):
                pool.wait_ge(mg.sig_f, h + 1)
                pool.tensor_tensor(o[:, 4 + h, :], o[:, 4 + h, :], sg[:, :], ALU.mult).then_inc(f_part, 1)

            step(Tile(N_GK))
            gla_forget(0)
            step(Tile(N_G))
            pool.wait_ge(f_part, 1)
            block_gates(mg, 0)
            gla_forget(1)
            step(Tile(N_G + 1))
            step(Tile(N_G + 2))
            gla_forget(2)
            gla_forget(3)
            step(Tile(N_G + 3))

            def gla(t, h):
                step(t)
                step(t.plus(1))
                power(mg.ms, h, mg.rs)
                step(t.plus(2))
                step(t.plus(3))
                pool.wait_ge(mg.o_done, h * 2)
                block_gates(mg, h)
                step(t.plus(4))
                gate(mg, 0, h * 2 - 1, h * 2 - 1, dyn(o, h * 2 - 2), h * 2 - 1)
                step(t.plus(5))
                gate(mg, 1, h * 2, h * 2, dyn(o, h * 2 - 1), h * 2)

            with pool.Fori(1, GH) as h:
                gla(Tile(N_G - 2, 6, h), h)
            step(Tile(N_GO - 2))
            power(mg.ms, GH, mg.rs)
            step(Tile(N_GO - 1))
            for j, factor in ((0, sg), (1, rms_x)):
                pool.wait_ge(mg.sig_g, 2 * GH - 1 + j)
                pool.tensor_tensor(factor[:, :], z[:, j, :], factor[:, :], ALU.mult).then_inc(mg.gs, 1)
            for j, factor in ((0, sg), (1, rms_x)):
                pool.wait_ge(mg.gs, 2 * GH - 1 + j)
                pool.wait_ge(mg.onorm, 2 * GH - 1 + j)
                o_last = o[:, 2 * GH - 2 + j, :]
                pool.tensor_tensor(o_last, o_last, factor[:, :], ALU.mult).then_inc(mg.gated, 1)
            to_x(N_GO)
            mlp(1, N_F1, 3)


_INS = ["x", "norm_mix", "norm_ffn", "hgrn_w_in", "hgrn_g_norm", "hgrn_w_out", "hgrn_lb_logits", "gla_w_in",
        "gla_w_gk_up", "gla_b_gk", "gla_g_norm", "gla_w_out", "ffn_w_gate_up", "ffn_w_down"]


def kernel(**inputs):
    import numpy as _np
    import concourse.bacc as _bacc
    from concourse import mybir as _mybir
    from concourse.bass_utils import run_bass_kernel_spmd as _run

    nc = _bacc.Bacc("TRN2", target_bir_lowering=False, num_devices=1)
    arrays, args = {}, []
    for name in _INS:
        a = _np.ascontiguousarray(inputs[name])
        arrays[f"in_{name}_dram"] = a
        args.append(nc.dram_tensor(f"in_{name}_dram", a.shape, _mybir.dt.from_np(a.dtype), kind="ExternalInput").ap())
    shape = tuple(int(s) for s in inputs["x"].shape)
    args.append(nc.dram_tensor("out_0_dram", shape, _mybir.dt.float32, kind="ExternalOutput").ap())
    trunk(nc, *args)
    r = _run(nc, [arrays], core_ids=[0])
    return r.results[0]["out_0_dram"]
```
